# Optimizing a Trainium2 kernel written in Bass

```python
import jax, jax.numpy as jnp
from jax import lax
import numpy as np

D_MODEL = 1024
BATCH = 1
SEQ = 128
DEPTH = 1
DEC_BATCH = 1
DEC_SEQ = 512
PAST_LEN = 128

GRID_W = 64
HEAD_DIM = 64
N_HEADS = D_MODEL // 128
N_KV_HEADS = N_HEADS // 4
KV_GROUP = N_HEADS // N_KV_HEADS
ATTN_CH = N_HEADS * HEAD_DIM
KV_CH = N_KV_HEADS * HEAD_DIM
CONV_CH = D_MODEL // 2
CONV_WIDTH = 31
POOL_WINDOWS = (2, 4, 8, 16)
POOL_GROUPS = 4
POOL_CH = D_MODEL // 2
POOL_GROUP_CH = POOL_CH // POOL_GROUPS
FOURIER_HEADS = 4
FOURIER_CH = D_MODEL // 2
FOURIER_HEAD_CH = FOURIER_CH // FOURIER_HEADS
MIX_WIDTH = ATTN_CH + CONV_CH + POOL_CH + FOURIER_CH
IN_COLS = ATTN_CH + 2 * KV_CH + 2 * CONV_CH + POOL_CH + FOURIER_CH
N_EXPERT_GROUPS = 4
EXPERTS_PER_GROUP = 4
N_EXPERTS = N_EXPERT_GROUPS * EXPERTS_PER_GROUP
TOP_K_IN_GROUP = 2
EXPERT_FF = D_MODEL // 4
ROPE_THETA = 10000.0
ROPE_PAIRS_PER_AXIS = HEAD_DIM // 4
Q_BLOCK = 128
EPS = 1e-6
N_MOD = 6

kernel_name = 'hybrid_flow_prefix_trunk_step'

def rms_norm(x, g):
    xf = x.astype(jnp.float32)
    y = xf * lax.rsqrt(jnp.mean(xf * xf, axis=-1, keepdims=True) + EPS)
    return (y * g.astype(jnp.float32)).astype(x.dtype)

def grid_rope(n_tokens):
    rows = n_tokens // GRID_W
    row = jnp.repeat(jnp.arange(rows), GRID_W).astype(jnp.float32)
    col = jnp.tile(jnp.arange(GRID_W), rows).astype(jnp.float32)
    inv = ROPE_THETA ** (-jnp.arange(ROPE_PAIRS_PER_AXIS, dtype=jnp.float32) / ROPE_PAIRS_PER_AXIS)
    ang = jnp.concatenate([row[:, None] * inv, col[:, None] * inv], axis=-1)
    return jnp.cos(ang)[:, None, :], jnp.sin(ang)[:, None, :]

def apply_rope(x, cos, sin):
    xf = x.astype(jnp.float32).reshape(*x.shape[:-1], HEAD_DIM // 2, 2)
    x0, x1 = xf[..., 0], xf[..., 1]
    out = jnp.stack([x0 * cos - x1 * sin, x0 * sin + x1 * cos], axis=-1)
    return out.reshape(x.shape).astype(x.dtype)

def gqa_attention(q, k, v):
    B, Lq = q.shape[0], q.shape[1]
    nb = Lq // Q_BLOCK
    qb = q.reshape(B, nb, Q_BLOCK, N_KV_HEADS, KV_GROUP, HEAD_DIM).transpose(1, 0, 2, 3, 4, 5)
    scale = HEAD_DIM ** -0.5

    def block(qblk):
        s = jnp.einsum('bqkgd,bskd->bkgqs', qblk, k).astype(jnp.float32) * scale
        p = jax.nn.softmax(s, axis=-1).astype(v.dtype)
        return jnp.einsum('bkgqs,bskd->bqkgd', p, v)

    o = lax.map(block, qb)
    return o.transpose(1, 0, 2, 3, 4, 5).reshape(B, Lq, ATTN_CH)

def conformer_conv(u2, w, b, ln_g, ln_b):
    a, gate = jnp.split(u2, 2, axis=-1)
    u = a * jax.nn.sigmoid(gate)
    y = lax.conv_general_dilated(u, w[:, None, :].astype(u.dtype), window_strides=(1,),
                                 padding=[(CONV_WIDTH // 2, CONV_WIDTH // 2)],
                                 dimension_numbers=('NWC', 'WIO', 'NWC'),
                                 feature_group_count=CONV_CH)
    yf = y.astype(jnp.float32) + b.astype(jnp.float32)
    mu = jnp.mean(yf, axis=-1, keepdims=True)
    var = jnp.mean(jnp.square(yf - mu), axis=-1, keepdims=True)
    yn = (yf - mu) * lax.rsqrt(var + EPS) * ln_g.astype(jnp.float32) + ln_b.astype(jnp.float32)
    return jax.nn.silu(yn).astype(u.dtype)

def multi_scale_pool(u, pool_w, pool_scale):
    B, L, _ = u.shape
    ug = u.reshape(B, L, POOL_GROUPS, POOL_GROUP_CH).astype(jnp.float32)
    cs = jnp.cumsum(ug, axis=1)
    cs = jnp.concatenate([jnp.zeros_like(cs[:, :1]), cs], axis=1)
    t = jnp.arange(L)
    outs = []
    for g, w in enumerate(POOL_WINDOWS):
        lo = jnp.clip(t - w // 2, 0, L)
        hi = jnp.clip(t + w - w // 2, 0, L)
        win_sum = cs[:, hi, g] - cs[:, lo, g]
        mean = win_sum / (hi - lo).astype(jnp.float32)[None, :, None]
        outs.append(mean - ug[:, :, g])
    pooled = jnp.stack(outs, axis=2).astype(u.dtype)
    mixed = jnp.einsum('blgc,gcd->blgd', pooled, pool_w)
    return mixed.reshape(B, L, POOL_CH) * pool_scale

def fourier_mix(u):
    B, L, _ = u.shape
    uh = u.reshape(B, L, FOURIER_HEADS, FOURIER_HEAD_CH).astype(jnp.float32)
    f = jnp.fft.fftn(uh, axes=(1, 3), norm='ortho').real
    return f.reshape(B, L, FOURIER_CH).astype(u.dtype)

def parallel_mixer(h, l, p, ctx_k, ctx_v, rope):
    B, L, _ = h.shape
    proj = h @ p['w_in'][l]
    o1 = ATTN_CH
    o2 = o1 + KV_CH
    o3 = o2 + KV_CH
    o4 = o3 + 2 * CONV_CH
    o5 = o4 + POOL_CH
    q, k, v, conv_in, pool_in, four_in = jnp.split(proj, [o1, o2, o3, o4, o5], axis=-1)
    q = rms_norm(q.reshape(B, L, N_HEADS, HEAD_DIM), p['q_norm'][l])
    k = rms_norm(k.reshape(B, L, N_KV_HEADS, HEAD_DIM), p['k_norm'][l])
    v = v.reshape(B, L, N_KV_HEADS, HEAD_DIM)
    if rope is None:
        keys, vals = k, v
    else:
        cos, sin = rope
        q = apply_rope(q, cos, sin)
        k_lat = apply_rope(k, cos, sin)
        keys = jnp.concatenate([ctx_k.astype(k.dtype), k_lat], axis=1)
        vals = jnp.concatenate([ctx_v.astype(v.dtype), v], axis=1)
    attn = gqa_attention(q, keys, vals)
    conv = conformer_conv(conv_in, p['conv_w'][l], p['conv_b'][l], p['conv_ln_g'][l], p['conv_ln_b'][l])
    pool = multi_scale_pool(pool_in, p['pool_w'][l], p['pool_scale'][l])
    four = fourier_mix(four_in)
    out = jnp.concatenate([attn, conv, pool, four], axis=-1) @ p['w_out'][l]
    return out, k, v

def hier_moe(h, l, p):
    B, L, D = h.shape
    T = B * L
    x = h.reshape(T, D)
    g_logits = (x @ p['router_group_w'][l] + p['router_group_b'][l]).astype(jnp.float32)
    g_prob = jax.nn.softmax(g_logits, axis=-1)
    g_idx = jnp.argmax(g_logits, axis=-1)
    g_w = jnp.take_along_axis(g_prob, g_idx[:, None], axis=-1)
    e_logits = (x @ p['router_expert_w'][l] + p['router_expert_b'][l]).astype(jnp.float32)
    e_logits = e_logits.reshape(T, N_EXPERT_GROUPS, EXPERTS_PER_GROUP)
    e_in = jnp.take_along_axis(e_logits, g_idx[:, None, None], axis=1)[:, 0]
    top_v, top_i = lax.top_k(e_in, TOP_K_IN_GROUP)
    top_p = jax.nn.softmax(top_v, axis=-1)
    local = jnp.sum(jax.nn.one_hot(top_i, EXPERTS_PER_GROUP, dtype=jnp.float32) * top_p[..., None], axis=1)
    gates = (jax.nn.one_hot(g_idx, N_EXPERT_GROUPS, dtype=jnp.float32)[:, :, None] * local[:, None, :])
    gates = gates.reshape(T, N_EXPERTS) * g_w
    hid = jax.nn.silu(jnp.einsum('td,edf->tef', x, p['moe_w_gate'][l])) * jnp.einsum('td,edf->tef', x, p['moe_w_up'][l])
    out = jnp.einsum('tef,efd->td', hid * gates[:, :, None].astype(hid.dtype), p['moe_w_down'][l])
    return out.reshape(B, L, D)

def trunk(x, cond, p, ctx_k_all, ctx_v_all, rope):
    ks, vs = [], []
    for l in range(DEPTH):
        mod = (jax.nn.silu(cond) @ p['w_ada'][l] + p['b_ada'][l])[:, None, :]
        sh1, sc1, g1, sh2, sc2, g2 = jnp.split(mod, N_MOD, axis=-1)
        hmix = rms_norm(x, p['norm_mix'][l]) * (1 + sc1) + sh1
        ctx_k = None if ctx_k_all is None else ctx_k_all[:, l]
        ctx_v = None if ctx_v_all is None else ctx_v_all[:, l]
        mix, k, v = parallel_mixer(hmix, l, p, ctx_k, ctx_v, rope)
        x = x + g1 * mix
        hffn = rms_norm(x, p['norm_ffn'][l]) * (1 + sc2) + sh2
        x = x + g2 * hier_moe(hffn, l, p)
        ks.append(k)
        vs.append(v)
    return rms_norm(x, p['final_norm']), ks, vs

def setup_inputs(seed: int = 0) -> dict:
    key = jax.random.key(seed)
    ks = jax.random.split(key, 32)
    f32 = jnp.float32
    D = D_MODEL

    def nrm(k, shape, scale):
        return jax.random.normal(k, shape, f32) * scale

    kv_shape = (DEC_BATCH, DEPTH, PAST_LEN, N_KV_HEADS, HEAD_DIM)
    return {
        'x_prompt': nrm(ks[0], (BATCH, SEQ, D), 1.0),
        'x_sample': nrm(ks[1], (DEC_BATCH, DEC_SEQ, D), 1.0),
        'cache_k': nrm(ks[2], kv_shape, 1.0),
        'cache_v': nrm(ks[3], kv_shape, 1.0),
        'c': nrm(ks[4], (DEC_BATCH, D), 1.0),
        'c_ctx': nrm(ks[5], (D,), 1.0),
        'w_ada': nrm(ks[6], (DEPTH, D, N_MOD * D), 0.5 * D ** -0.5),
        'b_ada': nrm(ks[7], (DEPTH, N_MOD * D), 0.02),
        'norm_mix': 1.0 + nrm(ks[8], (DEPTH, D), 0.02),
        'norm_ffn': 1.0 + nrm(ks[9], (DEPTH, D), 0.02),
        'w_in': nrm(ks[10], (DEPTH, D, IN_COLS), D ** -0.5),
        'w_out': nrm(ks[11], (DEPTH, MIX_WIDTH, D), MIX_WIDTH ** -0.5),
        'q_norm': 1.0 + nrm(ks[12], (DEPTH, HEAD_DIM), 0.02),
        'k_norm': 1.0 + nrm(ks[13], (DEPTH, HEAD_DIM), 0.02),
        'conv_w': nrm(ks[14], (DEPTH, CONV_WIDTH, CONV_CH), CONV_WIDTH ** -0.5),
        'conv_b': nrm(ks[15], (DEPTH, CONV_CH), 0.02),
        'conv_ln_g': 1.0 + nrm(ks[16], (DEPTH, CONV_CH), 0.02),
        'conv_ln_b': nrm(ks[17], (DEPTH, CONV_CH), 0.02),
        'pool_w': nrm(ks[18], (DEPTH, POOL_GROUPS, POOL_GROUP_CH, POOL_GROUP_CH), POOL_GROUP_CH ** -0.5),
        'pool_scale': 1.0 + nrm(ks[19], (DEPTH, POOL_CH), 0.1),
        'router_group_w': nrm(ks[20], (DEPTH, D, N_EXPERT_GROUPS), D ** -0.5),
        'router_group_b': nrm(ks[21], (DEPTH, N_EXPERT_GROUPS), 0.01),
        'router_expert_w': nrm(ks[22], (DEPTH, D, N_EXPERTS), D ** -0.5),
        'router_expert_b': nrm(ks[23], (DEPTH, N_EXPERTS), 0.01),
        'moe_w_gate': nrm(ks[24], (DEPTH, N_EXPERTS, D, EXPERT_FF), D ** -0.5),
        'moe_w_up': nrm(ks[25], (DEPTH, N_EXPERTS, D, EXPERT_FF), D ** -0.5),
        'moe_w_down': nrm(ks[26], (DEPTH, N_EXPERTS, EXPERT_FF, D), EXPERT_FF ** -0.5),
        'final_norm': 1.0 + nrm(ks[27], (D,), 0.02),
    }

def reference(x_prompt, x_sample, cache_k, cache_v, c, c_ctx, w_ada, b_ada, norm_mix, norm_ffn,
              w_in, w_out, q_norm, k_norm, conv_w, conv_b, conv_ln_g, conv_ln_b, pool_w, pool_scale,
              router_group_w, router_group_b, router_expert_w, router_expert_b,
              moe_w_gate, moe_w_up, moe_w_down, final_norm):
    p = {
        'w_ada': w_ada, 'b_ada': b_ada, 'norm_mix': norm_mix, 'norm_ffn': norm_ffn,
        'w_in': w_in, 'w_out': w_out, 'q_norm': q_norm, 'k_norm': k_norm,
        'conv_w': conv_w, 'conv_b': conv_b, 'conv_ln_g': conv_ln_g, 'conv_ln_b': conv_ln_b,
        'pool_w': pool_w, 'pool_scale': pool_scale,
        'router_group_w': router_group_w, 'router_group_b': router_group_b,
        'router_expert_w': router_expert_w, 'router_expert_b': router_expert_b,
        'moe_w_gate': moe_w_gate, 'moe_w_up': moe_w_up, 'moe_w_down': moe_w_down,
        'final_norm': final_norm,
    }
    y_prompt, ctx_ks, ctx_vs = trunk(x_prompt, c_ctx[None, :], p, None, None, None)
    new_cache_k = jnp.stack(ctx_ks, axis=1)
    new_cache_v = jnp.stack(ctx_vs, axis=1)
    rope = grid_rope(x_sample.shape[1])
    y_sample, _, _ = trunk(x_sample, c, p, cache_k, cache_v, rope)
    return (y_prompt, y_sample, new_cache_k, new_cache_v)


_drawn_inputs = setup_inputs


def setup_inputs(seed=0):
    import zlib

    import numpy as np

    out = dict(_drawn_inputs(seed))
    spreads = {}
    factors = {'cache_k': 8.0,
     'cache_v': 8.0,
     'norm_mix': 3.064,
     'norm_ffn': 4.735,
     'q_norm': 8.0,
     'k_norm': 2.81,
     'conv_b': 8.0,
     'conv_ln_g': 8.0,
     'conv_ln_b': 8.0,
     'pool_scale': 3.589,
     'router_group_b': 8.0,
     'router_expert_b': 21.829,
     'final_norm': 9.56}
    for name, (base, spread) in spreads.items():
        noise = np.random.default_rng([zlib.crc32(name.encode()), seed]).standard_normal(out[name].shape)
        drawn = base * np.exp(spread * noise) if base else spread * noise
        out[name] = __import__('jax').numpy.asarray(drawn.astype(out[name].dtype))
    for name, factor in factors.items():
        out[name] = (out[name] * factor).astype(out[name].dtype)
    return out
```

```python
from contextlib import ExitStack

import numpy as np

import concourse.bass as bass
from concourse import mybir

P = 128
D = 1024
KB = D // P
N_LAT, N_CTX = 512, 128
TOK = N_LAT + N_CTX
TT = TOK // P
LT = N_LAT // P
HEADS, KV, HD = 8, 2, 64
GRP = HEADS // KV
QKV = (HEADS + 2 * KV) * HD
TAPS = 31
HALF = TAPS // 2
CU = HALF + N_LAT + HALF + N_CTX + HALF
CY = N_LAT + HALF + N_CTX
WINDOWS = (2, 4, 8, 16)
PPAD = 8
PU = PPAD + N_LAT + PPAD + N_CTX + PPAD
NE, EPG, NG, FF = 16, 4, 4, 256
CH = 256
CHUNK = KB * CH
NRAW = 4
EPS = 1e-6
ADA1 = 2 * D // CH
ADA2 = 4 * D // CH
W_IN = [(0, KB, n, CH) for n in (768, 1280, 1024, 1536, 1792, 2048)]
W_IN += [(k, 4, n, 512) for n in (0, 2304) for k in (0, 4)] + [(0, KB, 512, CH)]
N_WIN = len(W_IN)
N_CHAN = 6
ROW_C, ROW_NMIX, ROW_NFFN, ROW_FIN, ROW_BADA, ROW_CB, ROW_LG, ROW_LB, ROW_PS = 0, 16, 24, 32, 40, 88, 92, 96, 100
N_ROWS = 104
C_ID, C_DCH, C_DPR, C_EDGE, N_CST = 0, 128, 384, 640, 768
R_U, R_TID, R_E, R_IOTA, N_RT = 0, 128, 136, 152, 168
N_OV = 10
NTILE = NE + N_OV


def build(nc, x_prompt, x_sample, cache_k, cache_v, c, c_ctx, w_ada, b_ada, norm_mix, norm_ffn, w_in, w_out,
          q_norm, k_norm, conv_w, conv_b, conv_ln_g, conv_ln_b, pool_w, pool_scale, router_group_w, router_group_b,
          router_expert_w, router_expert_b, moe_w_gate, moe_w_up, moe_w_down, final_norm,
          cst_d, rt_d, rope_d, dft_d, y_prompt, y_sample, new_k, new_v,
          mod_rows, h2_rows, slot_list, y_rows):
    f32, f32r, i32 = mybir.dt.float32, mybir.dt.float32r, mybir.dt.int32
    ALU, ACT, AX = mybir.AluOpType, mybir.ActivationFunctionType, mybir.AxisListType
    MUL, ADD, SUB = ALU.mult, ALU.add, ALU.subtract

    ZERO_SLOT = (ADA1 + N_WIN + ADA2 + 3) % NRAW

    RAW = 16512
    HL = RAW + 32768
    XT = HL + 32768
    R1 = XT + 20480
    R2 = R1 + 40960
    L = R2 + 40960
    SM = L + 40960
    place = [SM]

    def at(name, shape, off, dt=f32):
        return nc.alloc_sbuf_tensor_at(name, [P] + shape, dt, offset=off)

    def small(name, shape, dt=f32):
        n = 4
        for s in shape:
            n *= s
        place[0] += (-place[0]) % 32
        t = at(name, shape, place[0], dt)
        place[0] += n
        return t

    raw = [at(f"raw{s}", [CHUNK], RAW + 8192 * s) for s in range(NRAW)]
    w_hi = [at(f"w_hi{s}", [CHUNK], HL + 16384 * s, f32r) for s in range(2)]
    w_lo = [at(f"w_lo{s}", [CHUNK], HL + 16384 * s + 8192, f32r) for s in range(2)]
    x = at("x", [TT, D], XT)
    hT = at("hT", [KB, 2, TOK], R1, f32r)
    xs = at("xs", [TT, D], L)
    xn = at("xn", [KB, TOK], R2)
    hf = [at(f"hf{s}", [TOK], R2 + 26912 + 2560 * s) for s in range(2)]
    a1row = at("a1row", [2 * D], R2 + 32032)
    rows1 = at("rows1", [P], L + 35552)
    rows2 = at("rows2", [P], L + 36064)
    pool_u = at("pool_u", [4, PU], R2)
    pool_t = [at(f"pool_t{s}", [PU], R2 + 10624 + 2656 * s) for s in range(2)]
    cu = at("cu", [4, CU], R2 + 15936)
    cy = at("cy", [4, CY], R2 + 26912)
    gate_s = [at("gate_s0", [TOK], R2 + 37408), at("gate_s1", [TOK], L + 37888)]
    qkv = at("qkv", [TT, QKV], L)
    fu = at("fu", [TT, 512], L + 15360)
    qk_gain = at("qk_gain", [10 * HD], L + 25600)
    rope = at("rope", [LT, 2, HD // 2], L + 28160)
    rtmp = at("rtmp", [10 * HD], L + 29184)
    cst = at("cst", [N_CST], L + 31744)
    qtmp = at("qtmp", [10 * HD], L + 35552)
    dft = at("dft", [LT, 1024], HL)
    pool_wt = at("pool_wt", [4, P], HL + 16384)
    fpq = at("fpq", [4, 2, TOK], R1)
    arow = at("arow", [4 * D], R1 + 20480)
    frow = at("frow", [D], R1 + 36864)
    csq = at("csq", [4, CY], R2 + 15936)
    ln_v = at("ln_v", [CY], R2 + 10624)
    ln_r = at("ln_r", [CY], R2 + 10624 + 2656)
    mix1 = at("mix1", [KB, 2, TOK], R1, f32r)
    mix2 = at("mix2", [KB, 2, TOK], R2, f32r)
    kHL = at("kHL", [2, KV, 6 * P], HL, f32r)
    vs = at("vs", [6, 2, KV, 2, HD], HL + 12288, f32r)
    pb = [at(f"pb{s}", [5 * P], HL + 24576 + 2560 * s) for s in range(2)]
    ks = [at(f"ks{s}", [2, KV, 2, HD], HL + 24576 + 2048 * s, f32r) for s in range(2)]
    diag = [at(f"diag{s}", [P], HL + 29696 + 512 * s) for s in range(2)]
    ck, cv = at("ck", [KV * HD], HL + 31744), at("cv", [KV * HD], HL + 32256)
    ctxv = [at(f"ctxv{g}", [2, P], HL + 30720 + 1024 * g) for g in range(2)]
    qT = at("qT", [HEADS, P], L + 15360, f32r)
    pth = at("pth", [5, GRP, P], L + 19456, f32r)
    ptl = at("ptl", [5, GRP, P], L + 29696, f32r)
    qs = at("qs", [HEADS, 2, HD], L + 29696, f32r)
    g2t = at("g2t", [2, D], L)
    fint = at("fint", [D], L + 8192)
    gain2t = at("gain2t", [2, D], L + 12288)
    sh2t = at("sh2t", [2, D], L + 20480)
    g1t = at("g1t", [2, D], L + 28672)
    wr = at("wr", [KB, 20], L + 36864)
    rt = at("rt", [N_RT], L + 37504)
    rbias = at("rbias", [20], L + 38176)
    lgT = at("lgT", [TOK], L + 38272)
    h2k = [at(f"h2k{s}", [D], RAW + 16384 + 4096 * s) for s in range(2)]
    h2T = [at(f"h2T{s}", [KB, P], RAW + 24576 + 4096 * s) for s in range(2)]
    sq_out = [at(f"sq_out{s}", [D], RAW + 24576 + 4096 * s) for s in range(2)]
    zeros = at("zeros", [D], RAW + 8192 * ZERO_SLOT)
    rp = [R2 + 32768]

    def rsmall(name, shape, dt=f32):
        n = 4
        for s in shape:
            n *= s
        t = at(name, shape, rp[0], dt)
        rp[0] += n + (-n) % 32
        assert rp[0] <= R2 + 40960
        return t

    lg, eq, oh = rsmall("lg", [TT, 20]), rsmall("eq", [TT, 4]), rsmall("oh", [TT, 4])
    seen, e_in, oh1, oh2 = rsmall("seen", [TT, 1]), rsmall("e_in", [TT, 4]), rsmall("oh1", [TT, 4]), rsmall("oh2", [TT, 4])
    e2, ge4, eg = rsmall("e2", [TT, 4]), rsmall("ge4", [TT, 4]), rsmall("eg", [TT, NG, EPG])
    gm, m1, m2, gw, pe2, rden2 = (rsmall(n, [TT]) for n in ("gm", "m1", "m2", "gw", "pe2", "rden2"))
    A1, A2, AA = rsmall("A1", [TT, NG, EPG]), rsmall("A2", [TT, NG, EPG]), rsmall("AA", [TT, NG, EPG])
    tot, bt, rank = rsmall("tot", [TT, NE]), rsmall("bt", [TT, NE]), rsmall("rank", [TT, NE])
    fl, smap, cnt, n_ov = rsmall("fl", [TT, NE]), rsmall("smap", [TT, NE]), rsmall("cnt", [NE]), rsmall("n_ov", [NE])
    cum = [rsmall(f"cum{s}", [24]) for s in range(2)]
    c1, ovt, posf, npf = rsmall("c1", [NE]), rsmall("ovt", [N_OV, NE]), rsmall("posf", [2, TT]), rsmall("npf", [1])
    ovf = rsmall("ovf", [N_OV])
    tid = rsmall("tid", [TT], i32)
    m_raw = [at(f"m_raw{n}", [CHUNK], o) for n, o in enumerate((RAW, RAW + 8192, L + 28672, RAW + 16384, RAW + 24576, L + 12288))]
    gu_hi = [at(f"gu_hi{q}", [KB, 512], R, f32r) for q, R in enumerate((R1, R2))]
    gu_lo = [at(f"gu_lo{q}", [KB, 512], R + 16384, f32r) for q, R in enumerate((R1, R2))]
    xt_h = [at(f"xt_h{q}", [KB, P], R + 32768, f32r) for q, R in enumerate((R1, R2))]
    xt_l = [at(f"xt_l{q}", [KB, P], R + 36864, f32r) for q, R in enumerate((R1, R2))]
    d_hi, d_lo = at("d_hi", [2, D], HL, f32r), at("d_lo", [2, D], HL + 8192, f32r)
    xg = [at(f"xg{q}", [D], HL + 16384 + 4096 * q) for q in range(2)]
    sg, hid = at("sg", [FF], HL + 24576), at("hid", [FF], HL + 25600)
    ht_h, ht_l = at("ht_h", [2, P], HL + 26624, f32r), at("ht_l", [2, P], HL + 27648, f32r)
    ys = [at("ys0", [D], HL + 28672), at("ys1", [D], L + 20480)]
    ya = [at(f"ya{s}", [D], R1 + 8192 * s) for s in range(2)]
    yb = [at(f"yb{s}", [D], R1 + 8192 * s + 4096) for s in range(2)]
    yo = [at(f"yo{s}", [D], R2 + 4096 * s) for s in range(2)]
    ysq = [at(f"ysq{s}", [D], R2 + 8192 + 4096 * s) for s in range(2)]

    ident, ones = small("ident", [P]), small("ones", [P])
    vec, tapw = small("vec", [N_ROWS]), small("tapw", [TAPS * 4])
    condT = small("condT", [KB, 2])
    mods, gain1 = small("mods", [16, 2]), small("gain1", [KB, 2])
    ss, var_x, rs_x, nw = small("ss", [8]), small("var_x", [8]), small("rs_x", [8]), small("nw", [56])
    ss_qk, rs_qk = small("ss_qk", [50]), small("rs_qk", [50])
    smax, nbias, den, rden = (small(n, [8]) for n in ("smax", "nbias", "den", "rden"))
    gates, slots = small("gates", [2, TT]), small("slots", [2, TT], i32)
    idx, tile_e = small("idx", [NTILE], i32), small("tile_e", [NTILE], i32)
    idxc = [small(f"idxc{q}", [1], i32) for q in range(2)]
    npi, zero_i, ahead = small("npi", [1], i32), small("zero_i", [NTILE], i32), small("ahead", [8], i32)
    assert place[0] <= 229344, place[0]

    ctx = ExitStack()
    PS = ctx.enter_context(nc.psum_tensor("ps", [P, 4096], f32))

    def pair(n, w=TOK):
        return PS[:, 1024 * n:1024 * n + w]

    def bank(n, a=0, b=512):
        return PS[:, 512 * n + a:512 * n + b]

    def sem(name):
        return ctx.enter_context(nc.semaphore(name))

    def sems(names):
        return [sem(n) for n in names.split()]

    x_in = [sem(f"x_in{t}") for t in range(TT)]
    raw_in = [sem(f"raw_in{s}") for s in range(NRAW)]
    cst_in, rows_in, tabs_in, dft_in, poolw_in, cache_in, out_sent, zlist_in, tiles_in, g1_in, rt_in, arow_in = sems(
        "cst_in rows_in tabs_in dft_in poolw_in cache_in out_sent zlist_in tiles_in g1_in rt_in arow_in")
    dve_chain, pool_chain, act_chain = sems("dve_chain pool_chain act_chain")
    ones_set, rowsT, vec_made, cond_made, sq_made, var_made, rs_raw, xs_made, xT_ps, xn_made = sems(
        "ones_set rowsT vec_made cond_made sq_made var_made rs_raw xs_made xT_ps xn_made")
    ada_used, a1_made, a1T_ps, gain_made, hf_made, hhi_made, hlo_made = sems(
        "ada_used a1_made a1T_ps gain_made hf_made hhi_made hlo_made")
    hi_made, lo_made, win_used, pads_set, unit_ps, unit_out, glu_made, conv_made = sems(
        "hi_made lo_made win_used pads_set unit_ps unit_out glu_made conv_made")
    qk_var, qk_rsraw, qk_made, pooled_made, arow_fin, rows_sent = sems(
        "qk_var qk_rsraw qk_made pooled_made arow_fin rows_sent")
    sums_ps, mean_read, csq_made, fpq_ps, fpq_made, lnv_made, ln_raw, ln_app, silu_z, cmix_hi, cmix_lo = sems(
        "sums_ps mean_read csq_made fpq_ps fpq_made lnv_made ln_raw ln_app silu_z cmix_hi cmix_lo")
    pm_ps, pm_hi, pm_lo, fm_ps, fm_hi, fm_lo = sems("pm_ps pm_hi pm_lo fm_ps fm_hi fm_lo")
    khi_made, klo_made, vs_hi, vs_lo, kT_ps, kT_made = sems("khi_made klo_made vs_hi vs_lo kT_ps kT_made")
    qs_hi, qs_lo, qT_ps, qT_made, s_ps, nb_made, p_made, rd_made, diag_made, t_ps, pt_hi, pt_lo = sems(
        "qs_hi qs_lo qT_ps qT_made s_ps nb_made p_made rd_made diag_made t_ps pt_hi pt_lo")
    pv_ps, av_made, am_hi, am_lo, am_chain = sems("pv_ps av_made am_hi am_lo am_chain")
    wo_hi, wo_lo, wo_used, mo_ps, x2_made = sems(
        "wo_hi wo_lo wo_used mo_ps x2_made")
    h2_made, h2T_ps, h2T_made, lgT_ps, lgT_made, lg_ps = sems("h2_made h2T_ps h2T_made lgT_ps lgT_made lg_ps")
    h2_sent = [sem(f"h2_sent{s}") for s in range(2)]
    gsub_made, gexp_made, A_made, rank_ps, slots_made, list_sent, idx_in, np_made, first_lo = sems(
        "gsub_made gexp_made A_made rank_ps slots_made list_sent idx_in np_made first_lo")
    m_in = [sem(f"m_in{n}") for n in range(6)]
    xg_in = [sem(f"xg_in{q}") for q in range(2)]
    y_sent = [sem(f"y_sent{q}") for q in range(2)]
    g_hi, g_lo, u_hi, u_lo, dh_made, dl_made, xt_ps, xt_hi, xt_lo, gu_ps, sg_made, hid_made, ht_ps, ht_hi, ht_lo, dn_ps, ys_a, ys_b, idxc_made = sems(
        "g_hi g_lo u_hi u_lo dh_made dl_made xt_ps xt_hi xt_lo gu_ps sg_made hid_made ht_ps ht_hi ht_lo dn_ps ys_a ys_b idxc_made")
    ya_in = [sem(f"ya_in{s}") for s in range(2)]
    yo_sent = [sem(f"yo_sent{s}") for s in range(2)]
    ya_scaled, x3_made, yo_made = sems("ya_scaled x3_made yo_made")

    wa = w_ada[0].rearrange("(k p) n -> p k n", p=P)
    wi = w_in[0].rearrange("(k p) n -> p k n", p=P)
    wo = w_out[0].rearrange("(k p) n -> p k n", p=P)
    w_g = moe_w_gate[0].rearrange("e (k p) n -> p e k n", p=P)
    w_u = moe_w_up[0].rearrange("e (k p) n -> p e k n", p=P)
    w_d = moe_w_down[0].rearrange("e (f p) n -> p e f n", p=P)
    y_slots = y_rows.rearrange("(p s) n -> p s n", s=NTILE)
    A2_FIRST = ADA1 + N_WIN
    WO_FIRST = A2_FIRST + ADA2
    N_WO = 8

    def raw_count(n):
        return n % NRAW, 16 * (n // NRAW + 1)

    def wait_raw(eng, n):
        s, v = raw_count(n)
        eng.wait_ge(raw_in[s], v)
        return raw[s]

    UNIT_BANK = [2 * (u % 3) for u in range(2 * N_CHAN)] + [0, 1, 2, 3, 4] + [5, 6, 7, 0, 1] + [2, 3, 4, 5, 6]
    N_UNITS = len(UNIT_BANK)
    UNIT_WAIT = [max(u - 2, 0) for u in range(2 * N_CHAN)] + [10, 10, 11, 11, 12] + [12, 12, 12, 13, 14] + [15, 16, 17, 18, 19]

    def mixrow(k):
        return mix1[:, k] if k < 8 else mix2[:, 4 + k - 8] if k < 12 else mix2[:, k - 12]

    block = ctx.enter_context(nc.Block())

    @block.sync
    def _(sp):
        def chunk(n, src, k):
            s = n % NRAW
            sp.dma_start(raw[s][:, :].rearrange("p (k n) -> p k n", k=k), src).then_inc(raw_in[s], 16)

        def load_expert(e, n):
            for m, src in enumerate((w_g, w_u, w_d)):
                k = KB if m < 2 else 2
                sp.dma_start(m_raw[n + m][:, :].rearrange("p (k n) -> p k n", k=k),
                             src[:, bass.ds(e, 1), :, :].rearrange("p a k n -> p (a k) n")).then_inc(m_in[n + m], 16)

        for t in range(TT):
            sp.dma_start(x[:, t, :], x_sample[0, t * P:(t + 1) * P, :] if t < LT else x_prompt[0]).then_inc(x_in[t], 16)
        for n in range(A2_FIRST + NRAW):
            if NRAW <= n < ADA1 + NRAW:
                sp.wait_ge(ada_used, n - NRAW + 1)
            elif n >= ADA1 + NRAW:
                sp.wait_ge(lo_made, n - NRAW - ADA1 + 1)
            if n < ADA1:
                chunk(n, wa[:, :, n * CH:(n + 1) * CH], KB)
            elif n < A2_FIRST:
                k, nk, col, cols = W_IN[n - ADA1]
                chunk(n, wi[:, k:k + nk, col:col + cols], nk)
            else:
                a = n - A2_FIRST + ADA1
                chunk(n, wa[:, :, a * CH:(a + 1) * CH], KB)
        sp.wait_ge(unit_ps, N_UNITS)
        sp.dma_start(arow[0:2, :], b_ada[0, 2 * D:6 * D].partition_broadcast(2)).then_inc(arow_in, 16)
        sp.dma_start(frow[0:2, :], norm_ffn[0].partition_broadcast(2)).then_inc(arow_in, 16)
        sp.dma_start(dft[:, :, :], dft_d.rearrange("(t p) n -> p t n", p=P)).then_inc(dft_in, 16)
        sp.dma_start(pool_wt[:, :, :], pool_w[0].rearrange("g c d -> c g d")).then_inc(poolw_in, 16)
        with sp.Fori(1, ADA2 // NRAW) as r:
            for s in range(NRAW):
                sp.wait_ge(ada_used, r * NRAW + (ADA1 - NRAW + s + 1))
                chunk(A2_FIRST + s, wa[:, :, bass.ds(r * (NRAW * CH) + (ADA1 + s) * CH, CH)], KB)
        sp.wait_ge(qk_made, 1)
        sp.dma_start(new_k[0, 0].rearrange("s h d -> s (h d)"), qkv[:, LT, 512:640]).then_inc(out_sent, 16)
        sp.dma_start(new_v[0, 0].rearrange("s h d -> s (h d)"), qkv[:, LT, 640:768]).then_inc(out_sent, 16)
        for i in range(NRAW):
            sp.wait_ge(ada_used, ADA1 + ADA2 - NRAW + i + 1)
            n, cc = i // 4, i % 4
            if i == NRAW - 1:
                sp.wait_ge(zlist_in, 32)
            chunk(WO_FIRST + i, wo[:, 4 * cc:4 * cc + 4, n * 512:(n + 1) * 512], 4)
        sp.wait_ge(arow_fin, 1)
        sp.dma_start(mod_rows, arow[0:2, :]).then_inc(rows_sent, 16)
        sp.wait_ge(fm_lo, 4)
        sp.wait_ge(pm_lo, 4)
        sp.dma_start(ck[:, :], cache_k[0, 0].rearrange("s h d -> s (h d)")).then_inc(cache_in, 16)
        sp.dma_start(cv[:, :], cache_v[0, 0].rearrange("s h d -> s (h d)")).then_inc(cache_in, 16)

        sp.wait_ge(rows_sent, 16)
        sp.wait_ge(pv_ps, 2 * TT)
        row = mod_rows.rearrange("c (v n) -> c v n", v=4)
        for cnd in range(2):
            sp.dma_start(g1t[:, cnd, :], row[cnd, 0].partition_broadcast(P)).then_inc(g1_in, 16)
        for cnd in range(2):
            sp.dma_start(sh2t[:, cnd, :], row[cnd, 1].partition_broadcast(P)).then_inc(tiles_in, 16)
            sp.dma_start(gain2t[:, cnd, :], row[cnd, 2].partition_broadcast(P)).then_inc(tiles_in, 16)
            sp.dma_start(g2t[:, cnd, :], row[cnd, 3].partition_broadcast(P)).then_inc(tiles_in, 16)
        sp.dma_start(fint[:, :], final_norm.partition_broadcast(P)).then_inc(tiles_in, 16)
        sp.dma_start(wr[:, :, 0:4], router_group_w[0].rearrange("(k p) n -> p k n", p=P)).then_inc(rt_in, 16)
        sp.dma_start(wr[:, :, 4:20], router_expert_w[0].rearrange("(k p) n -> p k n", p=P)).then_inc(rt_in, 16)
        sp.dma_start(rt[:, :], rt_d).then_inc(rt_in, 16)
        sp.dma_start(rbias[:, 0:4], router_group_b[0].partition_broadcast(P)).then_inc(rt_in, 16)
        sp.dma_start(rbias[:, 4:20], router_expert_b[0].partition_broadcast(P)).then_inc(rt_in, 16)
        for i in range(NRAW, N_WO):
            sp.wait_ge(wo_lo, i - NRAW + 1)
            n, cc = i // 4, i % 4
            chunk(WO_FIRST + i, wo[:, 4 * cc:4 * cc + 4, n * 512:(n + 1) * 512], 4)
        for t in range(TT):
            sp.wait_ge(h2_made, t + 1)
            sp.dma_start(h2_rows[t * P:(t + 1) * P, :], h2k[t % 2][:, :]).then_inc(h2_sent[t % 2], 16)
            if t == 0:
                load_expert(0, 0)
        sp.wait_ge(lgT_ps, TT)
        for s in range(2):
            sp.wait_ge(h2_sent[s], 16 * ((TT - s + 1) // 2))
        load_expert(1, 3)
        sp.wait_ge(np_made, 1)
        sp.wait_ge(first_lo, 4)
        last = sp.value_load(npi[0:1, 0:1], min_val=NE // 2 - 1, max_val=(NE + 8) // 2)

        def tile(r, q, ahead):
            i = r * 2 + q
            if ahead:
                e = sp.value_load(tile_e[0:1, bass.ds(i + 2, 1)], min_val=0, max_val=NE - 1)
                sp.wait_ge(g_lo, i + 1)
                sp.wait_ge(u_lo, i + 1)
                sp.wait_ge(dl_made, i + 1)
                load_expert(e, 3 * q)
            sp.wait_ge(ys_a, i + 2)
            sp.wait_ge(ys_b, i + 2)
            sp.dma_start(y_slots[:, bass.ds(i, 1), :].rearrange("p a n -> p (a n)"), ys[q][:, :]).then_inc(y_sent[q], 16)

        with sp.Fori(0, last) as r:
            tile(r, 0, True)
            tile(r, 1, True)
        tile(last, 0, False)
        tile(last, 1, False)
        for s in range(2):
            sp.wait_ge(y_sent[s], last * 16 + 32)
        for t in range(TT):
            sp.wait_ge(yo_made, t + 1)
            sp.dma_start(y_sample[0, t * P:(t + 1) * P, :] if t < LT else y_prompt[0], yo[t % 2][:, :]).then_inc(yo_sent[t % 2], 16)
        for s in range(2):
            sp.wait_ge(yo_sent[s], 16 * ((TT - s + 1) // 2))
        sp.wait_ge(rows_sent, 16)
        sp.wait_ge(list_sent, 160)
        sp.wait_ge(zlist_in, 32)
        sp.wait_ge(out_sent, 32)

    @block.tensor
    def _(pe):
        pe.wait_ge(cst_in, 16)
        pe.wait_ge(rows_in, 16 * 11)
        idc = cst[:, C_ID:C_ID + P]
        pe.transpose(bank(7, 0, N_ROWS), rows1[0:N_ROWS, :], idc[0:N_ROWS, 0:N_ROWS])
        pe.transpose(bank(7, 128, 128 + 4 * TAPS), rows2[0:4 * TAPS, :], idc[0:4 * TAPS, 0:4 * TAPS]).then_inc(rowsT, 1)
        for k in range(KB):
            if k == 0:
                pe.wait_ge(xs_made, TT)
            if k >= 3:
                pe.wait_ge(xn_made, k - 2)
            for t in range(TT):
                tr = pe.transpose(pair(k % 3)[:, t * P:(t + 1) * P], xs[:, t, k * P:(k + 1) * P], idc)
            tr.then_inc(xT_ps, 1)

        def ada_chunk(w, out):
            for k in range(KB):
                mm = pe.matmul(out[0:2, 0:CH], condT[:, k, :], w[:, k * CH:(k + 1) * CH], start=(k == 0), stop=(k == KB - 1))
            mm.then_inc(ada_used, 1)

        pe.wait_ge(cond_made, 1)
        for n in range(ADA1):
            w = wait_raw(pe, n)
            if n >= 2:
                pe.wait_ge(a1_made, n - 1)
            ada_chunk(w, bank(6 + n % 2))
        pe.wait_ge(a1_made, ADA1)
        for b in range(16):
            tr = pe.transpose(bank(6, 2 * b, 2 * b + 2), a1row[0:2, b * P:(b + 1) * P], idc[0:2, 0:2])
        tr.then_inc(a1T_ps, 1)

        def split_mm(out, wh, wl, mh, ml, first, last):
            pe.matmul(out, wh, mh, start=first, stop=False)
            pe.matmul(out, wh, ml, start=False, stop=False)
            return pe.matmul(out, wl, mh, start=False, stop=last)

        pe.wait_ge(hlo_made, KB)
        unit = 0
        for j, (k0, nk, _, cols) in enumerate(W_IN):
            pe.wait_ge(lo_made, j + 1)
            hi = w_hi[j % 2][:, :].rearrange("p (k n) -> p k n", k=nk)
            lo = w_lo[j % 2][:, :].rearrange("p (k n) -> p k n", k=nk)
            ends = k0 + nk == KB
            for v in range(2 if j < N_CHAN else TT):
                u = unit + v
                if UNIT_WAIT[u] and k0 == 0:
                    pe.wait_ge(unit_out, UNIT_WAIT[u])
                for k in range(nk):
                    first, last = k0 + k == 0, k0 + k == KB - 1
                    if j < N_CHAN:
                        out = pair(u % 3)
                        wh, wl = hi[:, k, v * P:(v + 1) * P], lo[:, k, v * P:(v + 1) * P]
                        for a, b in ((0, N_LAT), (N_LAT, TOK)):
                            pe.matmul(out[:, a:b], wh, hT[:, k, 0, a:b], start=first, stop=False)
                            pe.matmul(out[:, a:b], wh, hT[:, k, 1, a:b], start=False, stop=False)
                        for a, b in ((N_LAT, TOK), (0, N_LAT)):
                            mm = pe.matmul(out[:, a:b], wl, hT[:, k, 0, a:b], start=False, stop=last)
                    else:
                        tok = slice(v * P, (v + 1) * P)
                        out = bank(UNIT_BANK[u], 0, cols)
                        mm = split_mm(out, hT[:, k0 + k, 0, tok], hT[:, k0 + k, 1, tok], hi[:, k, :], lo[:, k, :], first, last)
                if ends:
                    mm.then_inc(unit_ps, 1)
            if ends:
                unit += 2 if j < N_CHAN else TT
            else:
                mm.then_inc(win_used, 1)
        pe.wait_ge(unit_out, N_UNITS)
        with pe.Fori(0, ADA2 // NRAW) as r:
            for s in range(NRAW):
                slot, v = raw_count(A2_FIRST + s)
                pe.wait_ge(raw_in[slot], r * 16 + v)
                pe.wait_ge(a1_made, r * NRAW + (ADA1 + s - 1))
                ada_chunk(raw[slot], bank(6 + s % 2))
        pe.wait_ge(ones_set, 1)
        pe.wait_ge(conv_made, 4)

        def over_channels(out, rows):
            for blk in range(4):
                for a, b in ((0, 512), (512, CY)):
                    mm = pe.matmul(out[:, a:b], ones[:, :], rows[:, blk, a:b], start=(blk == 0), stop=(blk == 3))
            return mm

        over_channels(pair(0, CY), cy).then_inc(sums_ps, 1)
        pe.wait_ge(dft_in, 16)
        for n in range(8):
            h, part = n // 2, n % 2
            if n >= 3:
                pe.wait_ge(fpq_made, n - 2)
            if n == 2:
                pe.wait_ge(mean_read, 1)
            out = pair((1 + n) % 3)
            for t in range(LT):
                pe.matmul(out[:, 0:N_LAT], fu[:, t, h * P:(h + 1) * P], dft[:, t, part * 512:(part + 1) * 512], start=(t == 0), stop=(t == LT - 1))
            pe.matmul(out[:, N_LAT:TOK], fu[:, LT, h * P:(h + 1) * P], cst[:, C_DPR + part * P:C_DPR + (part + 1) * P],
                      start=True, stop=True).then_inc(fpq_ps, 1)
        pe.wait_ge(csq_made, 4)
        pe.wait_ge(fpq_made, 6)
        over_channels(pair(0, CY), csq).then_inc(sums_ps, 1)
        pe.wait_ge(poolw_in, 16)
        pe.wait_ge(pooled_made, 1)
        for g in range(4):
            if g < 2:
                pe.wait_ge(fpq_made, 7 + g)
            elif g == 2:
                pe.wait_ge(lnv_made, 1)
            else:
                pe.wait_ge(pm_lo, g - 2)
            out = pair((1 + g) % 3)
            pe.matmul(out[:, 0:N_LAT], pool_wt[:, g, :], pool_u[:, g, PPAD:PPAD + N_LAT], start=True, stop=True)
            pe.matmul(out[:, N_LAT:TOK], pool_wt[:, g, :], pool_u[:, g, 2 * PPAD + N_LAT:2 * PPAD + TOK], start=True, stop=True).then_inc(pm_ps, 1)
        for h in range(4):
            pe.wait_ge(pm_lo, min(h + 2, 4)) if h < 3 else pe.wait_ge(fm_lo, 1)
            out = pair((2 + h) % 3)
            for a, b in ((0, N_LAT), (N_LAT, TOK)):
                pe.matmul(out[:, a:b], cst[:, C_DCH:C_DCH + P], fpq[:, h, 0, a:b], start=True, stop=False)
                mm = pe.matmul(out[:, a:b], cst[:, C_DCH + P:C_DCH + 2 * P], fpq[:, h, 1, a:b], start=False, stop=True)
            mm.then_inc(fm_ps, 1)
        pe.wait_ge(fm_lo, 4)
        pe.wait_ge(a1_made, ADA1 + ADA2)
        for kt in range(6):
            pe.wait_ge(klo_made, kt + 1)
            if kt >= 2:
                pe.wait_ge(kT_made, kt - 1)
            for n in range(4):
                hl, j = n // 2, n % 2
                tr = pe.transpose(bank(4 + kt % 2, n * P, (n + 1) * P), ks[kt % 2][:, hl, j, :, :].rearrange("p a d -> p (a d)").bitcast(f32), ident[:, :])
            tr.then_inc(kT_ps, 1)
        pe.wait_ge(kT_made, 6)
        pe.wait_ge(vs_lo, 6)

        def attend(t, spans, key0, kt0, nkt):
            pe.wait_ge(qs_lo, t + 1)
            for h in range(HEADS):
                tr = pe.transpose(bank(4 + h // 4, (h % 4) * P, (h % 4 + 1) * P), qs[:, h, :, :].rearrange("p a d -> p (a d)").bitcast(f32), ident[:, :])
            tr.then_inc(qT_ps, 1)
            pe.wait_ge(qT_made, t + 1)

            def scores(h):
                if h >= 2:
                    pe.wait_ge(p_made, t * HEADS + (h - 1))
                out = pair(h % 2)
                for hl in range(2):
                    for a, b in spans:
                        mm = pe.matmul(out[:, a:b], qT[:, h, :], kHL[:, hl, h // GRP, key0 + a:key0 + b], start=(hl == 0), stop=(hl == 1))
                mm.then_inc(s_ps, 1)

            scores(0)
            scores(1)
            for h in range(HEADS):
                g = h // GRP
                pe.wait_ge(diag_made, t * HEADS + (h + 1))
                if h:
                    pe.wait_ge(pt_lo, t * HEADS + h)
                for kt in range(nkt):
                    tr = pe.matmul(pair(2)[:, kt * P:(kt + 1) * P], pb[h % 2][:, kt * P:(kt + 1) * P], diag[h % 2][:, :], start=True, stop=True)
                tr.then_inc(t_ps, 1)
                if h + 2 < HEADS:
                    scores(h + 2)
                if h % GRP == GRP - 1:
                    pe.wait_ge(pt_lo, t * HEADS + (h + 1))
                    out = bank(6 + g)
                    for kt in range(nkt):
                        ph = pth[:, kt, :, :].rearrange("p h q -> p (h q)")
                        pl = ptl[:, kt, :, :].rearrange("p h q -> p (h q)")
                        mm = split_mm(out, *(vs[:, kt0 + kt, hl, g, :, :].rearrange("p a d -> p (a d)") for hl in range(2)), ph, pl, kt == 0, kt == nkt - 1)
                    mm.then_inc(pv_ps, 1)

        with pe.Fori(0, LT) as t:
            attend(t, ((0, 512), (512, 640)), 0, 0, 5)
        attend(LT, ((0, P),), 5 * P, 5, 1)
        pe.wait_ge(am_lo, 2 * TT)
        for i in range(N_WO):
            n, cc = i // 4, i % 4
            pe.wait_ge(wo_lo, i + 1)
            hi = w_hi[i % 2][:, :].rearrange("p (k n) -> p k n", k=4)
            lo = w_lo[i % 2][:, :].rearrange("p (k n) -> p k n", k=4)
            for t in range(TT):
                if n and cc == 0 and t >= 3:
                    pe.wait_ge(x2_made, t - 2)
                tok = slice(t * P, (t + 1) * P)
                for kk in range(4):
                    m = mixrow(4 * cc + kk)
                    mm = split_mm(bank((5 * n + t) % 8), m[:, 0, tok], m[:, 1, tok], hi[:, kk, :], lo[:, kk, :], i % 4 == 0 and kk == 0, cc == 3 and kk == 3)
                if cc == 3:
                    mm.then_inc(mo_ps, 1)
            if cc < 3:
                mm.then_inc(wo_used, 1)
        pe.wait_ge(rt_in, 80)
        for t in range(TT):
            pe.wait_ge(h2_made, t + 1)
            for k in range(KB):
                tr = pe.transpose(pair(1 + t % 2, D)[:, k * P:(k + 1) * P], h2k[t % 2][:, k * P:(k + 1) * P], ident[:, :])
            tr.then_inc(h2T_ps, 1)
            pe.wait_ge(h2T_made, t + 1)
            if t >= 2:
                pe.wait_ge(lgT_made, t - 1)
            for k in range(KB):
                mm = pe.matmul(bank(6 + t % 2, 0, P)[0:20, :], wr[:, k, :], h2T[t % 2][:, k, :], start=(k == 0), stop=(k == KB - 1))
            mm.then_inc(lgT_ps, 1)
        for t in range(TT):
            pe.wait_ge(lgT_made, t + 1)
            tr = pe.transpose(bank(0, 20 * t, 20 * t + 20), lgT[0:20, t * P:(t + 1) * P], ident[0:20, 0:20])
        tr.then_inc(lg_ps, 1)
        pe.wait_ge(A_made, 1)
        used = AA[:, :, :, :].rearrange("p t g e -> p (t g e)")
        pe.matmul(bank(1, 0, TT * NE), rt[:, R_U:R_U + P], used, start=True, stop=True)
        pe.matmul(bank(1, 128, 128 + TT * NE), ones[:, :], used, start=True, stop=True).then_inc(rank_ps, 1)

        def tokens(n, r, q):
            pe.wait_ge(xg_in[q], r * 16 + 16)
            for k in range(KB):
                tr = pe.transpose(pair(0, D)[:, k * P:(k + 1) * P], xg[q][:, k * P:(k + 1) * P], ident[:, :])
            tr.then_inc(xt_ps, 1)

        def tile(r, q, more):
            i = r * 2 + q
            pe.wait_ge(u_lo, i + 1)
            pe.wait_ge(xt_lo, i + 1)
            for k in range(KB):
                mm = split_mm(bank(2 + q), xt_h[q][:, k, :], xt_l[q][:, k, :], gu_hi[q][:, k, :], gu_lo[q][:, k, :], k == 0, k == KB - 1)
            mm.then_inc(gu_ps, 1)
            if more:
                tokens(i + 1, r + q, 1 - q)
            pe.wait_ge(hid_made, i + 1)
            for f in range(2):
                tr = pe.transpose(bank(4, f * P, (f + 1) * P), hid[:, f * P:(f + 1) * P], ident[:, :])
            tr.then_inc(ht_ps, 1)
            pe.wait_ge(ht_lo, i + 1)
            pe.wait_ge(dl_made, i + 1)
            pe.wait_ge(ys_a, i + 1)
            pe.wait_ge(ys_b, i + 1)
            for f in range(2):
                for n in range(2):
                    half = slice(n * 512, (n + 1) * 512)
                    mm = split_mm(bank(6 + n), ht_h[:, f, :], ht_l[:, f, :], d_hi[:, f, half], d_lo[:, f, half], f == 0, f == 1)
            mm.then_inc(dn_ps, 1)

        pe.wait_ge(np_made, 1)
        last = pe.value_load(npi[0:1, 0:1], min_val=NE // 2 - 1, max_val=(NE + 8) // 2)
        tokens(0, 0, 0)
        pe.wait_ge(first_lo, 4)
        with pe.Fori(0, last) as r:
            tile(r, 0, True)
            tile(r, 1, True)
        tile(last, 0, True)
        tile(last, 1, False)

    @block.scalar
    def _(act):
        def link(ins, n=[0]):
            ins.then_inc(act_chain, 1)
            n[0] += 1
            act.wait_ge(act_chain, n[0])

        act.dma_start(cst[:, :], cst_d).then_inc(cst_in, 16)
        for row, src in ((ROW_C, c.rearrange("a (r p) -> (a r) p", p=P)),
                         (ROW_C + 8, c_ctx.rearrange("(r p) -> r p", p=P)),
                         (ROW_NMIX, norm_mix.rearrange("a (r p) -> (a r) p", p=P)),
                         (ROW_NFFN, norm_ffn.rearrange("a (r p) -> (a r) p", p=P)),
                         (ROW_FIN, final_norm.rearrange("(r p) -> r p", p=P)),
                         (ROW_BADA, b_ada.rearrange("a (r p) -> (a r) p", p=P)),
                         (ROW_CB, conv_b.rearrange("a (r p) -> (a r) p", p=P)),
                         (ROW_LG, conv_ln_g.rearrange("a (r p) -> (a r) p", p=P)),
                         (ROW_LB, conv_ln_b.rearrange("a (r p) -> (a r) p", p=P)),
                         (ROW_PS, pool_scale.rearrange("a (r p) -> (a r) p", p=P))):
            act.dma_start(rows1[row:row + src.shape[0], :], src).then_inc(rows_in, 16)
        act.dma_start(rows2[0:4 * TAPS, :], conv_w[0].rearrange("w (r p) -> (w r) p", p=P)).then_inc(rows_in, 16)
        for t in range(TT):
            act.wait_ge(x_in[t], 16)
            act.activation(xn[:, :, :].rearrange("p k n -> p (k n)")[:, t * D:(t + 1) * D], x[:, t, :], ACT.Square,
                           accum_out=ss[:, t:t + 1]).then_inc(sq_made, 1)
        act.wait_ge(var_made, 1)
        link(act.activation(rs_x[:, 0:TT], var_x[:, 0:TT], ACT.Ln))
        act.activation(rs_x[:, 0:TT], rs_x[:, 0:TT], ACT.Exp, scale=-0.5).then_inc(rs_raw, 1)
        act.wait_ge(vec_made, 1)
        act.activation(condT[:, :, :].rearrange("p k c -> p c k"), vec[:, ROW_C:ROW_C + 16].rearrange("p (c k) -> p c k", c=2),
                       ACT.Silu).then_inc(cond_made, 1)
        act.wait_ge(cst_in, 16)
        act.activation(ident[:, :], cst[:, C_ID:C_ID + P], ACT.Copy)
        for n in range(ADA1):
            act.wait_ge(ada_used, n + 1)
            act.activation(a1row[0:2, n * CH:(n + 1) * CH], bank(6 + n % 2)[0:2, 0:CH], ACT.Copy).then_inc(a1_made, 1)

        UNITS_AT = [2, 4, 6, 8, 10, 12, 12, 17, 17, 22, 27]

        def split_hi(j):
            act.wait_ge(raw_in[(ADA1 + j) % NRAW], raw_count(ADA1 + j)[1])
            if j >= 2:
                if W_IN[j - 2][0] + W_IN[j - 2][1] < KB:
                    act.wait_ge(win_used, 1 if j - 2 < 8 else 2)
                else:
                    act.wait_ge(unit_ps, UNITS_AT[j - 2])
            act.activation(w_hi[j % 2][:, :], raw[(ADA1 + j) % NRAW][:, :], ACT.Copy).then_inc(hi_made, 1)

        act.wait_ge(gain_made, 1)
        for k in range(KB):
            act.wait_ge(xn_made, k + 1)
            if k >= 2:
                act.wait_ge(hlo_made, k - 1)
            for cnd, (a, b) in enumerate(((0, N_LAT), (N_LAT, TOK))):
                act.activation(hf[k % 2][:, a:b], xn[:, k, a:b], ACT.Identity, bias=mods[:, k, cnd:cnd + 1],
                               scale=gain1[:, k, cnd:cnd + 1]).then_inc(hf_made, 1)
            act.wait_ge(hf_made, 2 * k + 2)
            act.activation(hT[:, k, 0, :], hf[k % 2][:, :], ACT.Copy).then_inc(hhi_made, 1)
            if k == 2:
                split_hi(0)
            if k == 5:
                split_hi(1)
        act.dma_start(rope[:, :, :, :].rearrange("p t a i -> p t (a i)"), rope_d.rearrange("(t p) i -> p t i", p=P)).then_inc(tabs_in, 16)
        for h in range(HEADS + KV):
            src = q_norm if h < HEADS else k_norm
            act.dma_start(qk_gain[:, h * HD:(h + 1) * HD], src[0].partition_broadcast(P)).then_inc(tabs_in, 16)
        act.wait_ge(pads_set, 2)
        unit = 0
        for j, (k0, nk, col, cols) in enumerate(W_IN):
            for v in range((2 if j < N_CHAN else TT) if k0 + nk == KB else 0):
                u = unit + v
                act.wait_ge(unit_ps, u + 1)
                if j < N_CHAN:
                    out = pair(u % 3)
                else:
                    out = bank(UNIT_BANK[u], 0, cols)
                if j in (0, 2):
                    blk = j + v
                    act.activation(cu[:, blk, HALF:HALF + N_LAT], out[:, 0:N_LAT], ACT.Copy)
                    act.activation(cu[:, blk, 2 * HALF + N_LAT:2 * HALF + TOK], out[:, N_LAT:TOK], ACT.Copy).then_inc(unit_out, 1)
                elif j in (1, 3):
                    blk = j - 1 + v
                    if blk >= 2:
                        act.wait_ge(glu_made, blk - 1)
                    act.activation(gate_s[blk % 2][:, :], out, ACT.Sigmoid).then_inc(unit_out, 1)
                elif j in (4, 5):
                    g = 2 * (j - 4) + v
                    act.activation(pool_u[:, g, PPAD:PPAD + N_LAT], out[:, 0:N_LAT], ACT.Copy)
                    act.activation(pool_u[:, g, 2 * PPAD + N_LAT:2 * PPAD + TOK], out[:, N_LAT:TOK], ACT.Copy).then_inc(unit_out, 1)
                elif j in (7, 10):
                    act.activation(qkv[:, v, col:col + cols], out, ACT.Copy).then_inc(unit_out, 1)
                else:
                    act.activation(fu[:, v, :], out, ACT.Copy).then_inc(unit_out, 1)
            if k0 + nk == KB:
                unit += 2 if j < N_CHAN else TT
            if j + 2 < N_WIN:
                split_hi(j + 2)
        act.wait_ge(qk_var, 1)
        link(act.activation(rs_qk[:, :], ss_qk[:, :], ACT.Ln))
        act.activation(rs_qk[:, :], rs_qk[:, :], ACT.Exp, scale=-0.5).then_inc(qk_rsraw, 1)
        for n in range(8):
            act.wait_ge(fpq_ps, n + 1)
            act.activation(fpq[:, n // 2, n % 2, :], pair((1 + n) % 3), ACT.Copy).then_inc(fpq_made, 1)
            if n == 3:
                for blk in range(4):
                    act.wait_ge(mean_read, blk + 1)
                    act.activation(csq[:, blk, :], cy[:, blk, :], ACT.Square).then_inc(csq_made, 1)
        act.wait_ge(lnv_made, 1)
        link(act.activation(ln_r[:, :], ln_v[:, :], ACT.Ln))
        act.activation(ln_r[:, :], ln_r[:, :], ACT.Exp, scale=-0.5).then_inc(ln_raw, 1)
        for blk in range(4):
            act.wait_ge(ln_app, blk + 1)
            if blk == 0:
                act.wait_ge(rows_sent, 16)
            if blk >= 2:
                act.wait_ge(cmix_lo, blk - 1)
            for a, b, o in ((0, N_LAT, 0), (N_LAT, TOK, HALF)):
                act.activation(gate_s[blk % 2][:, a:b], cy[:, blk, a + o:b + o], ACT.Silu, bias=vec[:, ROW_LB + blk:ROW_LB + blk + 1],
                               scale=vec[:, ROW_LG + blk:ROW_LG + blk + 1]).then_inc(silu_z, 1)
            act.wait_ge(silu_z, 2 * blk + 2)
            act.activation(mix1[:, 4 + blk, 0, :], gate_s[blk % 2][:, :], ACT.Copy).then_inc(cmix_hi, 1)
        act.wait_ge(cmix_lo, 4)
        for g in range(4):
            act.wait_ge(pm_ps, g + 1)
            act.activation(mix2[:, 4 + g, 0, :], pair((1 + g) % 3), ACT.Copy, scale=vec[:, ROW_PS + g:ROW_PS + g + 1]).then_inc(pm_hi, 1)
        for h in range(4):
            act.wait_ge(fm_ps, h + 1)
            act.activation(mix2[:, h, 0, :], pair((2 + h) % 3), ACT.Copy).then_inc(fm_hi, 1)
        act.wait_ge(qk_made, 5)
        act.wait_ge(fm_ps, 4)
        act.wait_ge(cache_in, 32)
        for kt in range(6):
            ksrc, vsrc = (ck[:, :], cv[:, :]) if kt == 0 else (qkv[:, kt - 1, 512:640], qkv[:, kt - 1, 640:768])
            if kt >= 2:
                act.wait_ge(kT_ps, kt - 1)
            act.activation(ks[kt % 2][:, 0, :, :, :], ksrc.rearrange("p (j d) -> p j d", j=KV).unsqueeze(2).broadcast_to([P, KV, 2, HD]),
                           ACT.Copy).then_inc(khi_made, 1)
            act.activation(vs[:, kt, 0, :, :, :], vsrc.rearrange("p (j d) -> p j d", j=KV).unsqueeze(2).broadcast_to([P, KV, 2, HD]),
                           ACT.Copy).then_inc(vs_hi, 1)
            if kt >= 1:
                act.wait_ge(kT_ps, kt)
                act.activation(kHL[:, :, :, (kt - 1) * P:kt * P].rearrange("p a j s -> p (a j) s"), bank(4 + (kt - 1) % 2).rearrange("p (n s) -> p n s", n=4), ACT.Copy).then_inc(kT_made, 1)
        act.wait_ge(kT_ps, 6)
        act.activation(kHL[:, :, :, 5 * P:6 * P].rearrange("p a j s -> p (a j) s"), bank(5).rearrange("p (n s) -> p n s", n=4), ACT.Copy).then_inc(kT_made, 1)

        def attend(t, w, nkt):
            act.activation(qs[:, :, 0, :], qkv[:, bass.ds(t, 1), 0:512].rearrange("p a (h d) -> p (a h) d", h=HEADS), ACT.Copy).then_inc(qs_hi, 1)
            act.wait_ge(qT_ps, t + 1)
            act.activation(qT[:, :, :].rearrange("p h q -> p (h q)"), pair(2, 1024), ACT.Copy).then_inc(qT_made, 1)

            def probs(h):
                act.wait_ge(nb_made, t * HEADS + (h + 1))
                if h >= 2:
                    act.wait_ge(t_ps, t * HEADS + (h - 1))
                act.activation(pb[h % 2][:, 0:w], pair(h % 2)[:, 0:w], ACT.Exp, bias=nbias[:, h:h + 1], scale=HD ** -0.5,
                               accum_out=den[:, h:h + 1]).then_inc(p_made, 1)

            probs(0)
            for h in range(HEADS):
                g = h // GRP
                if h + 1 < HEADS:
                    probs(h + 1)
                act.wait_ge(t_ps, t * HEADS + (h + 1))
                if h == GRP:
                    act.wait_ge(pv_ps, t * 2 + 1)
                act.activation(pth[:, 0:nkt, h % GRP, :], pair(2)[:, 0:nkt * P].rearrange("p (k s) -> p k s", k=nkt), ACT.Copy).then_inc(pt_hi, 1)
                if h % GRP == GRP - 1:
                    act.wait_ge(pv_ps, t * 2 + (g + 1))
                    v = bank(6 + g).rearrange("p (b o q) -> p b o q", b=2, o=2)
                    for o in range(2):
                        act.activation(ctxv[g][64 * o:64 * o + 64, :, :], v[64 * o:64 * o + 64, :, o, :], ACT.Copy).then_inc(av_made, 1)

        with act.Fori(0, LT) as t:
            attend(t, 640, 5)
        attend(LT, P, 1)

        def wo_split(i):
            act.wait_ge(raw_in[(WO_FIRST + i) % NRAW], raw_count(WO_FIRST + i)[1])
            if i == 0:
                act.wait_ge(pv_ps, 2 * TT)
            if i >= 2:
                j = i - 2
                if j % 4 < 3:
                    act.wait_ge(wo_used, 3 * (j // 4) + j % 4 + 1)
                else:
                    act.wait_ge(mo_ps, TT * (j // 4 + 1))
            act.activation(w_hi[i % 2][:, :], raw[(WO_FIRST + i) % NRAW][:, :], ACT.Copy).then_inc(wo_hi, 1)

        for i in range(N_WO):
            wo_split(i)
        act.wait_ge(mo_ps, 2 * TT)
        for t in range(TT):
            act.wait_ge(x2_made, TT + t + 1)
            if t >= 2:
                act.wait_ge(sq_made, TT + t - 1)
            act.activation(sq_out[t % 2][:, :], x[:, t, :], ACT.Square, accum_out=ss[:, t:t + 1]).then_inc(sq_made, 1)
        act.wait_ge(var_made, 2)
        link(act.activation(rs_x[:, 0:TT], var_x[:, 0:TT], ACT.Ln))
        act.activation(rs_x[:, 0:TT], rs_x[:, 0:TT], ACT.Exp, scale=-0.5).then_inc(rs_raw, 1)

        def gate_up_hi(q, count, u):
            act.wait_ge(m_in[3 * q + u], count)
            act.activation(gu_hi[q][:, :, u * FF:(u + 1) * FF], m_raw[3 * q + u][:, :].rearrange("p (k n) -> p k n", k=KB),
                           ACT.Copy).then_inc((g_hi, u_hi)[u], 1)

        def down_hi(q, count):
            act.wait_ge(m_in[3 * q + 2], count)
            act.activation(d_hi[:, :, :].rearrange("p f n -> p (f n)"), m_raw[3 * q + 2][:, :], ACT.Copy).then_inc(dh_made, 1)

        for t in range(TT):
            act.wait_ge(h2T_ps, t + 1)
            if t >= 2:
                act.wait_ge(lgT_ps, t - 1)
            act.activation(h2T[t % 2][:, :, :].rearrange("p k n -> p (k n)"), pair(1 + t % 2, D), ACT.Copy).then_inc(h2T_made, 1)
            act.wait_ge(lgT_ps, t + 1)
            act.activation(lgT[0:20, t * P:(t + 1) * P], bank(6 + t % 2, 0, P)[0:20, :], ACT.Copy).then_inc(lgT_made, 1)
        gate_up_hi(0, 16, 0)
        gate_up_hi(0, 16, 1)
        down_hi(0, 16)
        act.wait_ge(gsub_made, 1)
        act.activation(ge4[:, :, :], ge4[:, :, :], ACT.Exp).then_inc(gexp_made, 1)
        act.wait_ge(gsub_made, 2)
        act.activation(pe2[:, :], pe2[:, :], ACT.Exp).then_inc(gexp_made, 1)
        gate_up_hi(1, 16, 0)
        gate_up_hi(1, 16, 1)

        def tokens_hi(n, q):
            act.wait_ge(xt_ps, n + 1)
            act.activation(xt_h[q][:, :, :].rearrange("p k n -> p (k n)"), pair(0, D), ACT.Copy).then_inc(xt_hi, 1)

        def tile(r, q, more, ahead):
            i = r * 2 + q
            act.wait_ge(gu_ps, i + 1)
            act.activation(sg[:, :], bank(2 + q, 0, FF), ACT.Silu).then_inc(sg_made, 1)
            if more:
                tokens_hi(i + 1, 1 - q)
            act.wait_ge(ht_ps, i + 1)
            act.activation(ht_h[:, :, :].rearrange("p f n -> p (f n)"), bank(4, 0, FF), ACT.Copy).then_inc(ht_hi, 1)
            if ahead:
                gate_up_hi(q, r * 16 + 32, 0)
            act.wait_ge(dn_ps, i + 1)
            act.wait_ge(y_sent[q], r * 16 + 16)
            act.activation(ys[q][:, 0:512], bank(6), ACT.Copy).then_inc(ys_a, 1)
            if more:
                down_hi(1 - q, r * 16 + 16 + 16 * q)
            if ahead:
                gate_up_hi(q, r * 16 + 32, 1)

        act.wait_ge(np_made, 1)
        last = act.value_load(npi[0:1, 0:1], min_val=NE // 2 - 1, max_val=(NE + 8) // 2)
        tokens_hi(0, 0)
        with act.Fori(0, last) as r:
            tile(r, 0, True, True)
            tile(r, 1, True, True)
        tile(last, 0, True, False)
        tile(last, 1, False, False)

        def scale_first(t):
            act.wait_ge(ya_in[t % 2], 32 * (t // 2 + 1))
            act.activation(ya[t % 2][:, :], ya[t % 2][:, :], ACT.Copy, scale=gates[:, 0, t:t + 1]).then_inc(ya_scaled, 1)

        scale_first(0)
        for t in range(TT):
            if t + 1 < TT:
                scale_first(t + 1)
            act.wait_ge(x3_made, t + 1)
            if t >= 2:
                act.wait_ge(sq_made, 2 * TT + t - 1)
            act.activation(ysq[t % 2][:, :], x[:, t, :], ACT.Square, accum_out=ss[:, t:t + 1]).then_inc(sq_made, 1)
            act.wait_ge(var_made, 3 + t)
            link(act.activation(rs_x[:, t:t + 1], var_x[:, t:t + 1], ACT.Ln))
            act.activation(rs_x[:, t:t + 1], rs_x[:, t:t + 1], ACT.Exp, scale=-0.5).then_inc(rs_raw, 1)

    @block.gpsimd
    def _(pool):
        def link(ins, n=[0]):
            ins.then_inc(pool_chain, 1)
            n[0] += 1
            pool.wait_ge(pool_chain, n[0])

        for n, (s, v) in enumerate(((y_sent[0], 16), (y_sent[1], 16), (ys_a, 1), (ys_b, 1), (g_lo, 2), (u_lo, 2))):
            pool.memset(ahead[:, n:n + 1], 0).then_inc(s, v)
        pool.memset(ones[:, :], 1.0).then_inc(ones_set, 1)
        link(pool.memset(zero_i[:, :], 0))
        pool.dma_start(slot_list.rearrange("(p s) a -> p (s a)", p=P), zero_i[:, :]).then_inc(zlist_in, 16)

        def split_lo(j):
            pool.wait_ge(hi_made, j + 1)
            pool.tensor_tensor(w_lo[j % 2][:, :], raw[(ADA1 + j) % NRAW][:, :], w_hi[j % 2][:, :].bitcast(f32), SUB).then_inc(lo_made, 1)

        split_lo(0)
        pool.wait_ge(hlo_made, KB)
        pool.memset(cu[:, :, :], 0.0).then_inc(pads_set, 1)
        pool.memset(pool_u[:, :, :], 0.0).then_inc(pads_set, 1)
        for j in range(1, N_CHAN + 2):
            split_lo(j)
        for g, w in enumerate(WINDOWS):
            pool.wait_ge(unit_out, 8 + g + 1)
            src, have, a, b, s = pool_u[:, g, :], 1, 0, PU, 0
            while have < w:
                dst = pool_t[s][:, :]
                if have == 1:
                    a, b = 1, PU
                    link(pool.tensor_tensor(dst[:, a:b], src[:, a - 1:b - 1], src[:, a:b], ADD))
                else:
                    h = have // 2
                    a, b = a + h, b - h
                    link(pool.tensor_tensor(dst[:, a:b], src[:, a - h:b - h], src[:, a + h:b + h], ADD))
                src, have, s = dst, have * 2, 1 - s
            assert a <= PPAD and b >= PU - PPAD
            for q, (e, left) in enumerate(((PPAD, True), (PPAD + N_LAT, False), (2 * PPAD + N_LAT, True), (2 * PPAD + TOK, False))):
                n = w // 2
                e0 = e if left else e - n
                col = C_EDGE + (g * 4 + q) * 8
                link(pool.tensor_tensor(src[:, e0:e0 + n], src[:, e0:e0 + n], cst[:, col:col + n], MUL))
            mid = slice(PPAD, PU - PPAD)
            link(pool.tensor_scalar(src[:, mid], src[:, mid], 1.0 / w, None, MUL))
            ins = pool.tensor_tensor(pool_u[:, g, mid], src[:, mid], pool_u[:, g, mid], SUB)
            if g < 3:
                link(ins)
        ins.then_inc(pooled_made, 1)
        for j in range(N_CHAN + 2, N_WIN):
            split_lo(j)
        pool.wait_ge(ada_used, ADA1 + ADA2)
        link(pool.memset(zeros[:, :], 0.0))
        pool.dma_start(y_slots[:, NE:NTILE, :], zeros[:, :].unsqueeze(1).broadcast_to([P, N_OV, D])).then_inc(zlist_in, 16)

        pool.wait_ge(am_lo, 2 * TT)
        for i in range(N_WO):
            pool.wait_ge(wo_hi, i + 1)
            pool.tensor_tensor(w_lo[i % 2][:, :], raw[(WO_FIRST + i) % NRAW][:, :], w_hi[i % 2][:, :].bitcast(f32), SUB).then_inc(wo_lo, 1)
        def gate_up_lo(q, n, u):
            pool.wait_ge((g_hi, u_hi)[u], n + 1)
            cols = slice(u * FF, (u + 1) * FF)
            pool.tensor_tensor(gu_lo[q][:, :, cols], m_raw[3 * q + u][:, :].rearrange("p (k n) -> p k n", k=KB),
                               gu_hi[q][:, :, cols].bitcast(f32), SUB).then_inc(first_lo, 1)

        def down_lo(q):
            pool.tensor_tensor(d_lo[:, :, :].rearrange("p f n -> p (f n)"), m_raw[3 * q + 2][:, :],
                               d_hi[:, :, :].rearrange("p f n -> p (f n)").bitcast(f32), SUB).then_inc(dl_made, 1)

        def gather(q):
            pool.indirect_dma_start(xg[q][:, :], None, h2_rows, bass.IndirectOffsetOnAxis(ap=idxc[q][:, 0:1], axis=0)).then_inc(xg_in[q], 16)

        gate_up_lo(0, 0, 0)
        gate_up_lo(0, 0, 1)
        pool.wait_ge(dh_made, 1)
        down_lo(0)
        pool.wait_ge(rt_in, 80)
        link(pool.tensor_copy(tid[:, :], rt[:, R_TID:R_TID + TT]))
        pool.wait_ge(zlist_in, 16)
        pool.wait_ge(slots_made, 1)
        for a in range(2):
            for t in range(TT):
                pool.indirect_dma_start(slot_list, bass.IndirectOffsetOnAxis(ap=slots[:, a, t:t + 1], axis=0), tid[:, t:t + 1], None).then_inc(list_sent, 16)
        pool.wait_ge(list_sent, 160)
        pool.dma_start(idx[:, :], slot_list.rearrange("(p s) a -> p (s a)", p=P)).then_inc(idx_in, 16)
        pool.wait_ge(idx_in, 16)
        for s in range(2):
            pool.wait_ge(h2_sent[s], 16 * ((TT - s + 1) // 2))
        for q in range(2):
            pool.tensor_copy(idxc[q][:, :], idx[:, q:q + 1]).then_inc(idxc_made, 1)
            pool.wait_ge(idxc_made, q + 1)
            gather(q)
        gate_up_lo(1, 1, 0)
        gate_up_lo(1, 1, 1)
        pool.wait_ge(xt_ps, 1)
        pool.wait_ge(np_made, 1)
        last = pool.value_load(npi[0:1, 0:1], min_val=NE // 2 - 1, max_val=(NE + 8) // 2)

        def tile(r, q, more, ahead):
            i = r * 2 + q
            if ahead:
                pool.tensor_copy(idxc[q][:, :], idx[:, bass.ds(i + 2, 1)]).then_inc(idxc_made, 1)
                pool.wait_ge(idxc_made, i + 3)
            if more:
                pool.wait_ge(xt_ps, i + 2)
                pool.wait_ge(dh_made, i + 2)
                down_lo(1 - q)
            if ahead:
                gather(q)

        with pool.Fori(0, last) as r:
            tile(r, 0, True, True)
            tile(r, 1, True, True)
        tile(last, 0, True, False)
        for s in range(2):
            pool.wait_ge(y_sent[s], last * 16 + 32)
        pool.tensor_tensor(idxc[0][:, :], idx[:, 0:1], idx[:, 0:1], ADD).then_inc(idxc_made, 1)
        for t in range(TT):
            if t >= 2:
                pool.wait_ge(x3_made, t - 1)
            for a, y in ((0, ya), (1, yb)):
                pool.indirect_dma_start(y[t % 2][:, :], None, y_rows, bass.IndirectOffsetOnAxis(ap=slots[:, a, t:t + 1], axis=0)).then_inc(ya_in[t % 2], 16)

    @block.vector
    def _(dve):
        def link(ins, n=[0]):
            ins.then_inc(dve_chain, 1)
            n[0] += 1
            dve.wait_ge(dve_chain, n[0])

        def refine(y, v, tmp):
            link(dve.tensor_tensor(tmp, y, y, MUL))
            link(dve.tensor_tensor(tmp, tmp, v, MUL))
            link(dve.tensor_scalar(tmp, tmp, -0.5, 1.5, MUL, ADD))
            link(dve.tensor_tensor(y, y, tmp, MUL))

        dve.wait_ge(rowsT, 1)
        link(dve.tensor_copy(vec[:, :], bank(7, 0, N_ROWS)))
        dve.tensor_copy(tapw[:, :], bank(7, 128, 128 + 4 * TAPS)).then_inc(vec_made, 1)
        dve.wait_ge(sq_made, TT)
        dve.tensor_scalar(var_x[:, 0:TT], ss[:, 0:TT], 1.0 / D, EPS, MUL, ADD).then_inc(var_made, 1)
        dve.wait_ge(rs_raw, 1)
        refine(rs_x[:, 0:TT], var_x[:, 0:TT], nw[:, 0:TT])
        for t in range(TT):
            dve.tensor_scalar(xs[:, t, :], x[:, t, :], rs_x[:, t:t + 1], None, MUL).then_inc(xs_made, 1)
        for k in range(KB):
            dve.wait_ge(xT_ps, k + 1)
            dve.tensor_copy(xn[:, k, :], pair(k % 3)).then_inc(xn_made, 1)
        dve.wait_ge(a1T_ps, 1)
        link(dve.tensor_tensor(mods[:, :, :], bank(6, 0, 32).rearrange("p (b c) -> p b c", c=2),
                               vec[:, ROW_BADA:ROW_BADA + 16].unsqueeze(2).broadcast_to([P, 16, 2]), ADD))
        dve.scalar_tensor_tensor(out=gain1[:, :, :], in0=mods[:, 8:16, :], scalar=1.0,
                                 in1=vec[:, ROW_NMIX:ROW_NMIX + 8].unsqueeze(2).broadcast_to([P, 8, 2]), op0=ADD, op1=MUL).then_inc(gain_made, 1)
        for k in range(KB):
            dve.wait_ge(hhi_made, k + 1)
            dve.tensor_tensor(hT[:, k, 1, :], hf[k % 2][:, :], hT[:, k, 0, :].bitcast(f32), SUB).then_inc(hlo_made, 1)

        def glu(blk):
            dve.wait_ge(unit_out, 4 * (blk // 2) + 2 + blk % 2 + 1)
            link(dve.tensor_tensor(cu[:, blk, HALF:HALF + N_LAT], cu[:, blk, HALF:HALF + N_LAT], gate_s[blk % 2][:, 0:N_LAT], MUL))
            dve.tensor_tensor(cu[:, blk, 2 * HALF + N_LAT:2 * HALF + TOK], cu[:, blk, 2 * HALF + N_LAT:2 * HALF + TOK],
                              gate_s[blk % 2][:, N_LAT:TOK], MUL).then_inc(glu_made, 1)

        def conv(blk):
            dve.wait_ge(glu_made, blk + 1)
            link(dve.tensor_scalar(cy[:, blk, :], cu[:, blk, 0:CY], tapw[:, blk:blk + 1], vec[:, ROW_CB + blk:ROW_CB + blk + 1], MUL, ADD))
            for i in range(1, TAPS):
                ins = dve.scalar_tensor_tensor(out=cy[:, blk, :], in0=cu[:, blk, i:i + CY], scalar=tapw[:, 4 * i + blk:4 * i + blk + 1],
                                               in1=cy[:, blk, :], op0=MUL, op1=ADD)
                if i < TAPS - 1:
                    link(ins)
            ins.then_inc(conv_made, 1)

        glu(0)
        glu(1)
        conv(0)
        glu(2)
        glu(3)
        conv(1)
        conv(2)
        conv(3)
        dve.wait_ge(unit_out, N_UNITS)
        for t in range(TT):
            link(dve.tensor_tensor(qtmp[:, :], qkv[:, t, 0:640], qkv[:, t, 0:640], MUL))
            link(dve.tensor_reduce(ss_qk[:, 10 * t:10 * t + 10], qtmp[:, :].rearrange("p (h d) -> p h d", d=HD), AX.X, ADD))
        dve.tensor_scalar(ss_qk[:, :], ss_qk[:, :], 1.0 / HD, EPS, MUL, ADD).then_inc(qk_var, 1)
        dve.wait_ge(tabs_in, 16 * 11)
        dve.wait_ge(qk_rsraw, 1)
        refine(rs_qk[:, :], ss_qk[:, :], nw[:, 0:50])
        for t in (LT, 0, 1, 2, 3):
            heads = qkv[:, t, 0:640].rearrange("p (h d) -> p h d", d=HD)
            link(dve.tensor_tensor(heads, heads, rs_qk[:, 10 * t:10 * t + 10].unsqueeze(2).broadcast_to([P, 10, HD]), MUL))
            ins = dve.tensor_tensor(qkv[:, t, 0:640], qkv[:, t, 0:640], qk_gain[:, :], MUL)
            if t == LT:
                ins.then_inc(qk_made, 1)
                continue
            link(ins)
            two = qkv[:, t, 0:640].rearrange("p (h i a) -> p a h i", h=10, a=2)
            x0, x1 = two[:, 0], two[:, 1]
            cos = rope[:, t, 0:1, :].broadcast_to([P, 10, HD // 2])
            sin = rope[:, t, 1:2, :].broadcast_to([P, 10, HD // 2])
            tv = qtmp[:, :].rearrange("p (a h i) -> p a h i", a=2, h=10)
            zv = rtmp[:, :].rearrange("p (a h i) -> p a h i", a=2, h=10)
            if t:
                dve.wait_ge(qk_made, 1 + t)
            dve.tensor_tensor(tv[:, 0], x0, cos, MUL)
            dve.tensor_tensor(tv[:, 1], x1, sin, MUL)
            dve.tensor_tensor(zv[:, 0], x0, sin, MUL)
            link(dve.tensor_tensor(zv[:, 1], x1, cos, MUL))
            link(dve.tensor_tensor(x0, tv[:, 0], tv[:, 1], SUB))
            dve.tensor_tensor(x1, zv[:, 0], zv[:, 1], ADD).then_inc(qk_made, 1)
        dve.wait_ge(arow_in, 32)
        with dve.Fori(0, ADA2 // 2) as r:
            for s in range(2):
                dve.wait_ge(ada_used, r * 2 + (ADA1 + s + 1))
                cols = bass.ds(r * (2 * CH) + s * CH, CH)
                dve.tensor_tensor(arow[0:2, cols], arow[0:2, cols], bank(6 + s)[0:2, 0:CH], ADD).then_inc(a1_made, 1)
        dve.wait_ge(a1_made, ADA1 + ADA2)
        dve.scalar_tensor_tensor(out=arow[0:2, 2 * D:3 * D], in0=arow[0:2, 2 * D:3 * D], scalar=1.0, in1=frow[0:2, :], op0=ADD, op1=MUL).then_inc(arow_fin, 1)
        dve.wait_ge(sums_ps, 1)
        link(dve.tensor_scalar(ln_v[:, :], pair(0, CY), -1.0 / 512, None, MUL))
        for blk in range(4):
            dve.tensor_tensor(cy[:, blk, :], cy[:, blk, :], ln_v[:, :], ADD).then_inc(mean_read, 1)
        dve.wait_ge(sums_ps, 2)
        dve.wait_ge(mean_read, 4)
        dve.tensor_scalar(ln_v[:, :], pair(0, CY), 1.0 / 512, EPS, MUL, ADD).then_inc(lnv_made, 1)
        dve.wait_ge(lnv_made, 1)
        dve.wait_ge(ln_raw, 1)
        refine(ln_r[:, :], ln_v[:, :], csq[:, 0, :])
        for blk in range(4):
            dve.tensor_tensor(cy[:, blk, :], cy[:, blk, :], ln_r[:, :], MUL).then_inc(ln_app, 1)
        for blk in range(4):
            dve.wait_ge(cmix_hi, blk + 1)
            dve.tensor_tensor(mix1[:, 4 + blk, 1, :], gate_s[blk % 2][:, :], mix1[:, 4 + blk, 0, :].bitcast(f32), SUB).then_inc(cmix_lo, 1)
        for g in range(4):
            dve.wait_ge(pm_hi, g + 1)
            dve.scalar_tensor_tensor(out=mix2[:, 4 + g, 1, :], in0=pair((1 + g) % 3), scalar=vec[:, ROW_PS + g:ROW_PS + g + 1],
                                     in1=mix2[:, 4 + g, 0, :].bitcast(f32), op0=MUL, op1=SUB).then_inc(pm_lo, 1)
        for h in range(4):
            dve.wait_ge(fm_hi, h + 1)
            dve.tensor_tensor(mix2[:, h, 1, :], pair((2 + h) % 3), mix2[:, h, 0, :].bitcast(f32), SUB).then_inc(fm_lo, 1)
        for kt in range(6):
            ksrc, vsrc = (ck[:, :], cv[:, :]) if kt == 0 else (qkv[:, kt - 1, 512:640], qkv[:, kt - 1, 640:768])
            k2 = ksrc.rearrange("p (j d) -> p j d", j=KV)
            dve.wait_ge(khi_made, kt + 1)
            if kt >= 2:
                dve.wait_ge(kT_ps, kt - 1)
            for j in range(KV):
                ins = dve.tensor_tensor(ks[kt % 2][:, 1, j, :, :], k2[:, j:j + 1, :].broadcast_to([P, 2, HD]),
                                        ks[kt % 2][:, 0, j, :, :].bitcast(f32), SUB)
            ins.then_inc(klo_made, 1)
            dve.wait_ge(vs_hi, kt + 1)
            v2 = vsrc.rearrange("p (j d) -> p j d", j=KV)
            for j in range(KV):
                ins = dve.tensor_tensor(vs[:, kt, 1, j, :, :], v2[:, j:j + 1, :].broadcast_to([P, 2, HD]), vs[:, kt, 0, j, :, :].bitcast(f32), SUB)
            ins.then_inc(vs_lo, 1)

        def attend(t, w, nkt):
            dve.wait_ge(qs_hi, t + 1)
            dve.tensor_tensor(qs[:, :, 1, :], qkv[:, bass.ds(t, 1), 0:512].rearrange("p a (h d) -> p (a h) d", h=HEADS),
                              qs[:, :, 0, :].bitcast(f32), SUB).then_inc(qs_lo, 1)

            def bias(h):
                dve.wait_ge(s_ps, t * HEADS + (h + 1))
                dve.tensor_reduce(smax[:, h:h + 1], pair(h % 2)[:, 0:w], AX.X, ALU.max).then_inc(am_chain, 1)
                dve.wait_ge(am_chain, t * HEADS + (h + 1))
                dve.tensor_scalar(nbias[:, h:h + 1], smax[:, h:h + 1], -(HD ** -0.5), None, MUL).then_inc(nb_made, 1)

            bias(0)
            bias(1)
            for h in range(HEADS):
                g = h // GRP
                dve.wait_ge(p_made, t * HEADS + (h + 1))
                dve.reciprocal(rden[:, h:h + 1], den[:, h:h + 1]).then_inc(rd_made, 1)
                dve.wait_ge(rd_made, t * HEADS + (h + 1))
                dve.tensor_scalar(diag[h % 2][:, :], ident[:, :], rden[:, h:h + 1], None, MUL).then_inc(diag_made, 1)
                if h + 2 < HEADS:
                    bias(h + 2)
                dve.wait_ge(pt_hi, t * HEADS + (h + 1))
                dve.tensor_tensor(ptl[:, 0:nkt, h % GRP, :], pair(2)[:, 0:nkt * P].rearrange("p (k s) -> p k s", k=nkt),
                                  pth[:, 0:nkt, h % GRP, :].bitcast(f32), SUB).then_inc(pt_lo, 1)
                if h % GRP == GRP - 1:
                    cols = bass.ds(t * P, P)
                    hi, lo = (mix1[:, 2 * g:2 * g + 2, hl, cols] for hl in range(2))
                    dve.wait_ge(av_made, t * 4 + (2 * g + 2))
                    dve.tensor_scalar(hi, ctxv[g][:, :, :], 1.0, None, MUL).then_inc(am_hi, 1)
                    dve.wait_ge(am_hi, t * 2 + (g + 1))
                    dve.tensor_tensor(lo, ctxv[g][:, :, :], hi.bitcast(f32), SUB).then_inc(am_lo, 1)

        with dve.Fori(0, LT) as t:
            attend(t, 640, 5)
        attend(LT, P, 1)
        dve.wait_ge(g1_in, 32)
        for n in range(2):
            for t in range(TT):
                dve.wait_ge(mo_ps, TT * n + t + 1)
                half = slice(n * 512, (n + 1) * 512)
                b = bank((5 * n + t) % 8)
                link(dve.tensor_tensor(b, b, g1t[:, 0 if t < LT else 1, half], MUL))
                dve.tensor_tensor(x[:, t, half], x[:, t, half], b, ADD).then_inc(x2_made, 1)
        dve.wait_ge(sq_made, 2 * TT)
        dve.tensor_scalar(var_x[:, 0:TT], ss[:, 0:TT], 1.0 / D, EPS, MUL, ADD).then_inc(var_made, 1)
        dve.wait_ge(rs_raw, 2)
        refine(rs_x[:, 0:TT], var_x[:, 0:TT], nw[:, 0:TT])
        dve.wait_ge(tiles_in, 7 * 16)
        for t in range(TT):
            cnd = 0 if t < LT else 1
            if t >= 2:
                dve.wait_ge(h2_sent[t % 2], 16 * (t // 2))
                dve.wait_ge(h2T_ps, t - 1)
            link(dve.scalar_tensor_tensor(out=h2k[t % 2][:, :], in0=x[:, t, :], scalar=rs_x[:, t:t + 1], in1=gain2t[:, cnd, :], op0=MUL, op1=MUL))
            dve.tensor_tensor(h2k[t % 2][:, :], h2k[t % 2][:, :], sh2t[:, cnd, :], ADD).then_inc(h2_made, 1)

        def first_of(dst, flags):
            link(dve.tensor_copy(seen[:, :, :], flags[:, :, 0:1]))
            dve.tensor_copy(dst[:, :, 0:1], flags[:, :, 0:1])
            for j in range(1, 4):
                link(dve.tensor_tensor(dst[:, :, j:j + 1], flags[:, :, j:j + 1], seen[:, :, :], ALU.is_gt))
                if j < 3:
                    link(dve.tensor_tensor(seen[:, :, :], seen[:, :, :], flags[:, :, j:j + 1], ALU.max))

        def wide(v, n=4):
            return v[:, :].unsqueeze(2).broadcast_to([P, TT, n])

        dve.wait_ge(rt_in, 80)
        dve.wait_ge(lg_ps, 1)
        link(dve.tensor_tensor(lg[:, :, :], bank(0, 0, TT * 20).rearrange("p (t n) -> p t n", t=TT),
                               rbias[:, :].unsqueeze(1).broadcast_to([P, TT, 20]), ADD))
        gl, el = lg[:, :, 0:4], lg[:, :, 4:20].rearrange("p t (g e) -> p t g e", g=NG)
        link(dve.tensor_reduce(gm[:, :], gl, AX.X, ALU.max))
        dve.tensor_tensor(ge4[:, :, :], gl, wide(gm), SUB).then_inc(gsub_made, 1)
        link(dve.tensor_tensor(eq[:, :, :], gl, wide(gm), ALU.is_equal))
        first_of(oh, eq)
        link(dve.tensor_tensor(eg[:, :, :, :], el, oh[:, :, :].unsqueeze(3).broadcast_to([P, TT, NG, EPG]), MUL))
        link(dve.tensor_reduce(e_in[:, :, :], eg[:, :, :, :].rearrange("p t g e -> p t e g"), AX.X, ADD))
        link(dve.tensor_reduce(m1[:, :], e_in[:, :, :], AX.X, ALU.max))
        link(dve.tensor_tensor(eq[:, :, :], e_in[:, :, :], wide(m1), ALU.is_equal))
        first_of(oh1, eq)
        link(dve.scalar_tensor_tensor(out=e2[:, :, :], in0=oh1[:, :, :], scalar=-3e38, in1=e_in[:, :, :], op0=MUL, op1=ADD))
        link(dve.tensor_reduce(m2[:, :], e2[:, :, :], AX.X, ALU.max))
        dve.tensor_tensor(pe2[:, :], m2[:, :], m1[:, :], SUB).then_inc(gsub_made, 1)
        link(dve.tensor_tensor(eq[:, :, :], e2[:, :, :], wide(m2), ALU.is_equal))
        first_of(oh2, eq)
        for A, o in ((A1, oh1), (A2, oh2)):
            link(dve.tensor_tensor(A[:, :, :, :], oh[:, :, :].unsqueeze(3).broadcast_to([P, TT, NG, EPG]),
                                   o[:, :, :].unsqueeze(2).broadcast_to([P, TT, NG, EPG]), MUL))
        dve.tensor_tensor(AA[:, :, :, :], A1[:, :, :, :], A2[:, :, :, :], ADD).then_inc(A_made, 1)
        dve.wait_ge(gexp_made, 1)
        link(dve.tensor_reduce(gw[:, :], ge4[:, :, :], AX.X, ADD))
        link(dve.reciprocal(gw[:, :], gw[:, :]))
        dve.wait_ge(gexp_made, 2)
        link(dve.tensor_scalar(rden2[:, :], pe2[:, :], 1.0, None, ADD))
        link(dve.reciprocal(rden2[:, :], rden2[:, :]))
        link(dve.tensor_tensor(gates[:, 0, :], rden2[:, :], gw[:, :], MUL))
        dve.tensor_tensor(gates[:, 1, :], gates[:, 0, :], pe2[:, :], MUL)
        dve.wait_ge(rank_ps, 1)
        link(dve.tensor_copy(tot[:, :, :], bank(1, 128, 128 + TT * NE).rearrange("p (t n) -> p t n", t=TT)))
        link(dve.memset(bt[:, 0, :], 0.0))
        for t in range(1, TT):
            link(dve.tensor_tensor(bt[:, t, :], bt[:, t - 1, :], tot[:, t - 1, :], ADD))
        link(dve.tensor_tensor(cnt[:, :], bt[:, TT - 1, :], tot[:, TT - 1, :], ADD))
        link(dve.tensor_tensor(rank[:, :, :], bank(1, 0, TT * NE).rearrange("p (t n) -> p t n", t=TT), bt[:, :, :], ADD))
        for s in range(2):
            link(dve.memset(cum[s][:, 0:8], 0.0))
        ovf_n = cum[0][:, 8:24]
        link(dve.tensor_scalar(ovf_n, cnt[:, :], 128.5, None, ALU.is_ge))
        for m in range(2, TT):
            link(dve.scalar_tensor_tensor(out=ovf_n, in0=cnt[:, :], scalar=m * P + 0.5, in1=ovf_n, op0=ALU.is_ge, op1=ADD))
        link(dve.tensor_copy(n_ov[:, :], ovf_n))
        for n, d in enumerate((1, 2, 4, 8)):
            a, b = cum[n % 2], cum[1 - n % 2]
            link(dve.tensor_tensor(b[:, 8:24], a[:, 8:24], a[:, 8 - d:24 - d], ADD))
        ov_incl = cum[0][:, 8:24]
        link(dve.tensor_scalar(ovf[:, :], rt[:, R_IOTA:R_IOTA + N_OV], ov_incl[:, NE - 1:NE], None, ALU.is_lt))
        link(dve.tensor_reduce(npf[:, :], ovf[:, :].rearrange("p (o a) -> p a o", a=2)[:, 0:1, :], AX.X, ADD))
        link(dve.tensor_scalar(npf[:, :], npf[:, :], NE / 2 - 1.0, None, ADD))
        dve.tensor_copy(npi[:, :], npf[:, :])
        link(dve.tensor_tensor(ovt[:, :, :], ov_incl.unsqueeze(1).broadcast_to([P, N_OV, NE]),
                               rt[:, R_IOTA:R_IOTA + N_OV].unsqueeze(2).broadcast_to([P, N_OV, NE]), ALU.is_le))
        link(dve.tensor_reduce(ovf[:, :], ovt[:, :, :], AX.X, ADD))
        link(dve.tensor_scalar(ovf[:, :], ovf[:, :], float(NE - 1), None, ALU.min))
        dve.tensor_copy(tile_e[:, NE:NTILE], ovf[:, :])
        dve.tensor_copy(tile_e[:, 0:NE], rt[:, R_E:R_E + NE]).then_inc(np_made, 1)
        link(dve.tensor_scalar(fl[:, :, :], rank[:, :, :], float(P), None, ALU.is_ge))
        for m in range(2, TT):
            link(dve.scalar_tensor_tensor(out=fl[:, :, :], in0=rank[:, :, :], scalar=float(m * P), in1=fl[:, :, :], op0=ALU.is_ge, op1=ADD))
        link(dve.tensor_tensor(c1[:, :], ov_incl, n_ov[:, :], SUB))
        link(dve.tensor_tensor(c1[:, :], c1[:, :], rt[:, R_E:R_E + NE], SUB))
        link(dve.tensor_scalar(c1[:, :], c1[:, :], float(NE - 1), None, ADD))
        link(dve.tensor_scalar(smap[:, :, :], fl[:, :, :], 1.0, None, ALU.is_ge))
        link(dve.tensor_tensor(smap[:, :, :], smap[:, :, :], c1[:, :].unsqueeze(1).broadcast_to([P, TT, NE]), MUL))
        link(dve.scalar_tensor_tensor(out=smap[:, :, :], in0=fl[:, :, :], scalar=1.0 - P * NTILE, in1=smap[:, :, :], op0=MUL, op1=ADD))
        link(dve.scalar_tensor_tensor(out=smap[:, :, :], in0=rank[:, :, :], scalar=float(NTILE), in1=smap[:, :, :], op0=MUL, op1=ADD))
        link(dve.tensor_tensor(smap[:, :, :], smap[:, :, :], rt[:, R_E:R_E + NE].unsqueeze(1).broadcast_to([P, TT, NE]), ADD))
        for a, A in enumerate((A1, A2)):
            flat = A[:, :, :, :].rearrange("p t g e -> p t (g e)")
            link(dve.tensor_tensor(flat, flat, smap[:, :, :], MUL))
            link(dve.tensor_reduce(posf[:, a, :], flat, AX.X, ADD))
        dve.tensor_copy(slots[:, :, :], posf[:, :, :]).then_inc(slots_made, 1)

        def gate_up_lo(q, n, u):
            dve.wait_ge((g_hi, u_hi)[u], n + 1)
            cols = slice(u * FF, (u + 1) * FF)
            dve.tensor_tensor(gu_lo[q][:, :, cols], m_raw[3 * q + u][:, :].rearrange("p (k n) -> p k n", k=KB),
                              gu_hi[q][:, :, cols].bitcast(f32), SUB).then_inc((g_lo, u_lo)[u], 1)

        def tokens_lo(n, q):
            dve.wait_ge(xt_hi, n + 1)
            dve.tensor_tensor(xt_l[q][:, :, :].rearrange("p k n -> p (k n)"), pair(0, D),
                              xt_h[q][:, :, :].rearrange("p k n -> p (k n)").bitcast(f32), SUB).then_inc(xt_lo, 1)

        def tile(r, q, more, ahead):
            i = r * 2 + q
            dve.wait_ge(sg_made, i + 1)
            dve.tensor_tensor(hid[:, :], sg[:, :], bank(2 + q, FF, 2 * FF), MUL).then_inc(hid_made, 1)
            if more:
                tokens_lo(i + 1, 1 - q)
            dve.wait_ge(ht_hi, i + 1)
            dve.tensor_tensor(ht_l[:, :, :].rearrange("p f n -> p (f n)"), bank(4, 0, FF),
                              ht_h[:, :, :].rearrange("p f n -> p (f n)").bitcast(f32), SUB).then_inc(ht_lo, 1)
            if ahead:
                gate_up_lo(q, i + 2, 0)
            dve.wait_ge(dn_ps, i + 1)
            dve.wait_ge(y_sent[q], r * 16 + 16)
            dve.tensor_copy(ys[q][:, 512:D], bank(7)).then_inc(ys_b, 1)
            if ahead:
                gate_up_lo(q, i + 2, 1)

        dve.wait_ge(np_made, 1)
        last = dve.value_load(npi[0:1, 0:1], min_val=NE // 2 - 1, max_val=(NE + 8) // 2)
        tokens_lo(0, 0)
        with dve.Fori(0, last) as r:
            tile(r, 0, True, True)
            tile(r, 1, True, True)
        tile(last, 0, True, False)
        tile(last, 1, False, False)

        def combine(t):
            cnd = 0 if t < LT else 1
            dve.wait_ge(ya_scaled, t + 1)
            link(dve.scalar_tensor_tensor(out=ya[t % 2][:, :], in0=yb[t % 2][:, :], scalar=gates[:, 1, t:t + 1], in1=ya[t % 2][:, :], op0=MUL, op1=ADD))
            link(dve.tensor_tensor(ya[t % 2][:, :], ya[t % 2][:, :], g2t[:, cnd, :], MUL))
            dve.tensor_tensor(x[:, t, :], x[:, t, :], ya[t % 2][:, :], ADD).then_inc(x3_made, 1)

        def finish(t):
            col = slice(t, t + 1)
            dve.wait_ge(sq_made, 2 * TT + t + 1)
            dve.tensor_scalar(var_x[:, col], ss[:, col], 1.0 / D, EPS, MUL, ADD).then_inc(var_made, 1)
            dve.wait_ge(rs_raw, 3 + t)
            refine(rs_x[:, col], var_x[:, col], nw[:, col])
            if t >= 2:
                dve.wait_ge(yo_sent[t % 2], 16 * (t // 2))
            dve.scalar_tensor_tensor(out=yo[t % 2][:, :], in0=x[:, t, :], scalar=rs_x[:, col], in1=fint[:, :], op0=MUL, op1=MUL).then_inc(yo_made, 1)

        combine(0)
        for t in range(TT):
            if t + 1 < TT:
                combine(t + 1)
            finish(t)

    ctx.close()


def constants():
    p = np.arange(P)
    cst = np.zeros((P, N_CST), np.float32)
    cst[:, C_ID:C_ID + P] = np.eye(P)
    ang = 2 * np.pi * np.outer(p, p) / P
    cst[:, C_DCH:C_DCH + P] = np.cos(ang)
    cst[:, C_DCH + P:C_DCH + 2 * P] = -np.sin(ang)
    cst[:, C_DPR:C_DPR + P] = np.cos(ang) / P
    cst[:, C_DPR + P:C_DPR + 2 * P] = np.sin(ang) / P
    for g, w in enumerate(WINDOWS):
        n = w // 2
        for q in range(4):
            length = N_LAT if q < 2 else N_CTX
            for i in range(n):
                t = i if q % 2 == 0 else length - n + i
                cnt = min(t + w - n, length) - max(t - n, 0)
                cst[:, C_EDGE + (g * 4 + q) * 8 + i] = w / cnt
    rt = np.zeros((P, N_RT), np.float32)
    rt[:, R_U:R_U + P] = p[:, None] < p[None, :]
    rt[:, R_TID:R_TID + TT] = p[:, None] + P * np.arange(TT)
    rt[:, R_E:R_E + NE] = np.arange(NE)
    rt[:, R_IOTA:R_IOTA + N_OV] = np.arange(N_OV)
    n = np.arange(N_LAT)
    inv = (np.float32(10000.0) ** (-np.arange(HD // 4, dtype=np.float32) / np.float32(HD // 4))).astype(np.float32)
    ang = np.concatenate([(n // 64).astype(np.float32)[:, None] * inv, (n % 64).astype(np.float32)[:, None] * inv], axis=1)
    rope = np.concatenate([np.cos(ang), np.sin(ang)], axis=1).astype(np.float32)
    th = 2 * np.pi * (np.outer(n, n) % N_LAT) / N_LAT
    scale = 1.0 / np.sqrt(N_LAT * P)
    dft = np.concatenate([np.cos(th) * scale, np.sin(th) * scale], axis=1).astype(np.float32)
    return {"cst": cst, "rt": rt, "rope": rope, "dft": dft}


_INS = ['x_prompt', 'x_sample', 'cache_k', 'cache_v', 'c', 'c_ctx', 'w_ada', 'b_ada', 'norm_mix', 'norm_ffn', 'w_in',
        'w_out', 'q_norm', 'k_norm', 'conv_w', 'conv_b', 'conv_ln_g', 'conv_ln_b', 'pool_w', 'pool_scale',
        'router_group_w', 'router_group_b', 'router_expert_w', 'router_expert_b', 'moe_w_gate', 'moe_w_up',
        'moe_w_down', 'final_norm']
_OUTS = [(1, N_CTX, D), (1, N_LAT, D), (1, 1, N_CTX, KV, HD), (1, 1, N_CTX, KV, HD)]


def kernel(**inputs):
    import concourse.bacc as _bacc
    from concourse.bass_utils import run_bass_kernel_spmd as _run

    nc = _bacc.Bacc("TRN2", target_bir_lowering=False, num_devices=1)
    arrays, args = {}, []
    tables = constants()
    for name, a in [(n, inputs[n]) for n in _INS] + list(tables.items()):
        a = np.ascontiguousarray(a)
        arrays[f"in_{name}_dram"] = a
        args.append(nc.dram_tensor(f"in_{name}_dram", a.shape, mybir.dt.from_np(a.dtype), kind="ExternalInput").ap())
    for i, shape in enumerate(_OUTS):
        args.append(nc.dram_tensor(f"out_{i}_dram", shape, mybir.dt.float32, kind="ExternalOutput").ap())
    for name, shape, dt in (("mod_rows", (2, 4 * D), mybir.dt.float32), ("h2_rows", (TOK, D), mybir.dt.float32),
                            ("slot_list", (P * NTILE, 1), mybir.dt.int32), ("y_rows", (P * NTILE, D), mybir.dt.float32)):
        args.append(nc.dram_tensor(name, shape, dt, kind="Internal").ap())
    build(nc, *args)
    r = _run(nc, [arrays], core_ids=[0])
    return tuple(r.results[0][f"out_{i}_dram"] for i in range(len(_OUTS)))
```

```python
from contextlib import ExitStack

import numpy as np

import concourse.bass as bass
from concourse import mybir

P = 128
D = 1024
KB = D // P
N_LAT, N_CTX = 512, 128
TOK = N_LAT + N_CTX
TT = TOK // P
LT = N_LAT // P
HEADS, KV, HD = 8, 2, 64
GRP = HEADS // KV
QKV = (HEADS + 2 * KV) * HD
TAPS = 31
HALF = TAPS // 2
CU = HALF + N_LAT + HALF + N_CTX + HALF
CY = N_LAT + HALF + N_CTX
WINDOWS = (2, 4, 8, 16)
PPAD = 8
PU = PPAD + N_LAT + PPAD + N_CTX + PPAD
NE, EPG, NG, FF = 16, 4, 4, 256
CH = 256
CHUNK = KB * CH
NRAW = 4
EPS = 1e-6
ADA1 = 2 * D // CH
ADA2 = 4 * D // CH
W_IN = [(0, KB, n, CH) for n in (768, 1280, 1024, 1536, 1792, 2048)]
W_IN += [(k, 4, n, 512) for n in (0, 2304) for k in (0, 4)] + [(0, KB, 512, CH)]
N_WIN = len(W_IN)
N_CHAN = 6
ROW_C, ROW_NMIX, ROW_NFFN, ROW_FIN, ROW_BADA, ROW_CB, ROW_LG, ROW_LB, ROW_PS = 0, 16, 24, 32, 40, 88, 92, 96, 100
N_ROWS = 104
C_ID, C_DCH, C_DPR, C_EDGE, N_CST = 0, 128, 384, 640, 768
R_U, R_TID, R_E, R_IOTA, N_RT = 0, 128, 136, 152, 168
N_OV = 10
NTILE = NE + N_OV


def build(nc, x_prompt, x_sample, cache_k, cache_v, c, c_ctx, w_ada, b_ada, norm_mix, norm_ffn, w_in, w_out,
          q_norm, k_norm, conv_w, conv_b, conv_ln_g, conv_ln_b, pool_w, pool_scale, router_group_w, router_group_b,
          router_expert_w, router_expert_b, moe_w_gate, moe_w_up, moe_w_down, final_norm,
          cst_d, rt_d, rope_d, dft_d, y_prompt, y_sample, new_k, new_v,
          mod_rows, h2_rows, slot_list, y_rows):
    f32, f32r, i32 = mybir.dt.float32, mybir.dt.float32r, mybir.dt.int32
    ALU, ACT, AX = mybir.AluOpType, mybir.ActivationFunctionType, mybir.AxisListType
    MUL, ADD, SUB = ALU.mult, ALU.add, ALU.subtract

    ZERO_SLOT = (ADA1 + N_WIN + ADA2 + 3) % NRAW

    RAW = 16512
    HL = RAW + 32768
    XT = HL + 32768
    R1 = XT + 20480
    R2 = R1 + 40960
    L = R2 + 40960
    SM = L + 40960
    place = [SM]

    def at(name, shape, off, dt=f32):
        return nc.alloc_sbuf_tensor_at(name, [P] + shape, dt, offset=off)

    def small(name, shape, dt=f32):
        n = 4
        for s in shape:
            n *= s
        place[0] += (-place[0]) % 32
        t = at(name, shape, place[0], dt)
        place[0] += n
        return t

    raw = [at(f"raw{s}", [CHUNK], RAW + 8192 * s) for s in range(NRAW)]
    w_hi = [at(f"w_hi{s}", [CHUNK], HL + 16384 * s, f32r) for s in range(2)]
    w_lo = [at(f"w_lo{s}", [CHUNK], HL + 16384 * s + 8192, f32r) for s in range(2)]
    x = at("x", [TT, D], XT)
    hT = at("hT", [KB, 2, TOK], R1, f32r)
    xs = at("xs", [TT, D], L)
    xn = at("xn", [KB, TOK], R2)
    hf = [at(f"hf{s}", [TOK], R2 + 26912 + 2560 * s) for s in range(2)]
    a1row = at("a1row", [2 * D], R2 + 32032)
    rows1 = at("rows1", [P], L + 35552)
    rows2 = at("rows2", [P], L + 36064)
    pool_u = at("pool_u", [4, PU], R2)
    pool_t = [at(f"pool_t{s}", [PU], R2 + 10624 + 2656 * s) for s in range(2)]
    cu = at("cu", [4, CU], R2 + 15936)
    cy = at("cy", [4, CY], R2 + 26912)
    gate_s = [at("gate_s0", [TOK], R2 + 37408), at("gate_s1", [TOK], L + 37888)]
    qkv = at("qkv", [TT, QKV], L)
    fu = at("fu", [TT, 512], L + 15360)
    qk_gain = at("qk_gain", [10 * HD], L + 25600)
    rope = at("rope", [LT, 2, HD // 2], L + 28160)
    rtmp = at("rtmp", [10 * HD], L + 29184)
    cst = at("cst", [N_CST], L + 31744)
    qtmp = at("qtmp", [10 * HD], L + 35552)
    dft = at("dft", [LT, 1024], HL)
    pool_wt = at("pool_wt", [4, P], HL + 16384)
    fpq = at("fpq", [4, 2, TOK], R1)
    arow = at("arow", [4 * D], R1 + 20480)
    brow = at("brow", [4 * D], R1)
    frow = at("frow", [D], R1 + 36864)
    csq = at("csq", [4, CY], R2 + 15936)
    ln_v = at("ln_v", [CY], R2 + 10624)
    ln_r = at("ln_r", [CY], R2 + 10624 + 2656)
    mix1 = at("mix1", [KB, 2, TOK], R1, f32r)
    mix2 = at("mix2", [KB, 2, TOK], R2, f32r)
    kHL = at("kHL", [2, KV, 6 * P], HL, f32r)
    vs = at("vs", [6, 2, KV, 2, HD], HL + 12288, f32r)
    pb = [at(f"pb{s}", [5 * P], HL + 24576 + 2560 * s) for s in range(2)]
    ks = [at(f"ks{s}", [2, KV, 2, HD], HL + 24576 + 2048 * s, f32r) for s in range(2)]
    diag = [at(f"diag{s}", [P], HL + 29696 + 512 * s) for s in range(2)]
    ck, cv = at("ck", [KV * HD], HL + 31744), at("cv", [KV * HD], HL + 32256)
    ctxv = [at(f"ctxv{g}", [2, P], HL + 30720 + 1024 * g) for g in range(2)]
    qT = at("qT", [HEADS, P], L + 15360, f32r)
    pth = at("pth", [5, GRP, P], L + 19456, f32r)
    ptl = at("ptl", [5, GRP, P], L + 29696, f32r)
    qs = at("qs", [HEADS, 2, HD], RAW + 8192 * ZERO_SLOT, f32r)
    g2t = at("g2t", [2, D], L)
    fint = at("fint", [D], L + 8192)
    gain2t = at("gain2t", [2, D], L + 12288)
    sh2t = at("sh2t", [2, D], L + 20480)
    g1t = at("g1t", [2, D], L + 28672)
    wr = at("wr", [KB, 20], L + 36864)
    rt = at("rt", [N_RT], L + 37504)
    rbias = at("rbias", [20], L + 38176)
    lgT = at("lgT", [TOK], L + 38272)
    h2k = [at(f"h2k{t}", [D], o) for t, o in enumerate((RAW + 16384, RAW + 20480, HL + 16384, HL + 20480, HL + 24576))]
    h2T = [at(f"h2T{s}", [KB, P], RAW + 24576 + 4096 * s) for s in range(2)]
    sq_out = [at(f"sq_out{s}", [D], RAW + 24576 + 4096 * s) for s in range(2)]
    zeros = at("zeros", [D], RAW + 8192 * ZERO_SLOT)
    rp = [R2 + 32768]

    def rsmall(name, shape, dt=f32):
        n = 4
        for s in shape:
            n *= s
        t = at(name, shape, rp[0], dt)
        rp[0] += n + (-n) % 32
        assert rp[0] <= R2 + 40960
        return t

    lg, eq, oh = rsmall("lg", [TT, 20]), rsmall("eq", [TT, 4]), rsmall("oh", [TT, 4])
    seen, e_in, oh1, oh2 = rsmall("seen", [TT, 1]), rsmall("e_in", [TT, 4]), rsmall("oh1", [TT, 4]), rsmall("oh2", [TT, 4])
    e2, ge4, eg = rsmall("e2", [TT, 4]), rsmall("ge4", [TT, 4]), rsmall("eg", [TT, NG, EPG])
    gm, m1, m2, gw, pe2, rden2 = (rsmall(n, [TT]) for n in ("gm", "m1", "m2", "gw", "pe2", "rden2"))
    A1, A2, AA = rsmall("A1", [TT, NG, EPG]), rsmall("A2", [TT, NG, EPG]), rsmall("AA", [TT, NG, EPG])
    tot, bt, rank = rsmall("tot", [TT, NE]), rsmall("bt", [TT, NE]), rsmall("rank", [TT, NE])
    fl, smap, cnt, n_ov = rsmall("fl", [TT, NE]), rsmall("smap", [TT, NE]), rsmall("cnt", [NE]), rsmall("n_ov", [NE])
    cum = [rsmall(f"cum{s}", [24]) for s in range(2)]
    c1, ovt, posf, npf = rsmall("c1", [NE]), rsmall("ovt", [N_OV, NE]), rsmall("posf", [2, TT]), rsmall("npf", [1])
    ovf = rsmall("ovf", [N_OV])
    tid = rsmall("tid", [TT], i32)
    m_raw = [at(f"m_raw{n}", [CHUNK], o) for n, o in enumerate((RAW, RAW + 8192, L + 28672, RAW + 16384, RAW + 24576, L + 12288))]
    gu_hi = [at(f"gu_hi{q}", [KB, 512], R, f32r) for q, R in enumerate((R1, R2))]
    gu_lo = [at(f"gu_lo{q}", [KB, 512], R + 16384, f32r) for q, R in enumerate((R1, R2))]
    xt_h = [at(f"xt_h{q}", [KB, P], R + 32768, f32r) for q, R in enumerate((R1, R2))]
    xt_l = [at(f"xt_l{q}", [KB, P], R + 36864, f32r) for q, R in enumerate((R1, R2))]
    d_hi, d_lo = at("d_hi", [2, D], HL, f32r), at("d_lo", [2, D], HL + 8192, f32r)
    xg = [at(f"xg{q}", [D], HL + 16384 + 4096 * q) for q in range(2)]
    sg, hid = at("sg", [FF], HL + 24576), at("hid", [FF], HL + 25600)
    ht_h = [at(f"ht_h{q}", [2, P], (HL + 26624, L + 24576)[q], f32r) for q in range(2)]
    ht_l = [at(f"ht_l{q}", [2, P], (HL + 27648, L + 25600)[q], f32r) for q in range(2)]
    ys = [at("ys0", [D], HL + 28672), at("ys1", [D], L + 20480)]
    ya = [at(f"ya{t}", [D], R1 + 8192 * t) for t in range(TT)]
    yb = [at(f"yb{t}", [D], R1 + 8192 * t + 4096) for t in range(TT)]
    yo = [at(f"yo{s}", [D], R2 + 4096 * s) for s in range(2)]
    ysq = [at(f"ysq{s}", [D], R2 + 8192 + 4096 * s) for s in range(2)]

    ident, ones = small("ident", [P]), small("ones", [P])
    vec, tapw = small("vec", [N_ROWS]), small("tapw", [TAPS * 4])
    condT = small("condT", [KB, 2])
    mods, gain1 = small("mods", [16, 2]), small("gain1", [KB, 2])
    ss, var_x, rs_x, nw = small("ss", [8]), small("var_x", [8]), small("rs_x", [8]), small("nw", [56])
    ss_qk, rs_qk = small("ss_qk", [50]), small("rs_qk", [50])
    smax, nbias, den, rden = (small(n, [8]) for n in ("smax", "nbias", "den", "rden"))
    gates, slots = small("gates", [2, TT]), small("slots", [2, TT], i32)
    idx, tile_e = small("idx", [NTILE], i32), small("tile_e", [NTILE + 2], i32)
    idxc = [small(f"idxc{q}", [1], i32) for q in range(2)]
    npi, zero_i, ahead = small("npi", [1], i32), small("zero_i", [NTILE], i32), small("ahead", [8], i32)
    assert place[0] <= 229344, place[0]

    ctx = ExitStack()
    PS = ctx.enter_context(nc.psum_tensor("ps", [P, 4096], f32))

    def pair(n, w=TOK):
        return PS[:, 1024 * n:1024 * n + w]

    def bank(n, a=0, b=512):
        return PS[:, 512 * n + a:512 * n + b]

    def sem(name):
        return ctx.enter_context(nc.semaphore(name))

    def sems(names):
        return [sem(n) for n in names.split()]

    x_in = [sem(f"x_in{t}") for t in range(TT)]
    raw_in = [sem(f"raw_in{s}") for s in range(NRAW)]
    cst_in, rows_in, tabs_in, dft_in, poolw_in, cache_in, out_sent, zlist_in, tiles_in, g1_in, rt_in, arow_in = sems(
        "cst_in rows_in tabs_in dft_in poolw_in cache_in out_sent zlist_in tiles_in g1_in rt_in arow_in")
    dve_chain, pool_chain = sems("dve_chain pool_chain")
    ones_set, rowsT, vec_made, cond_made, sq_made, var_made, rs_raw, xs_made, xT_ps, xn_made = sems(
        "ones_set rowsT vec_made cond_made sq_made var_made rs_raw xs_made xT_ps xn_made")
    ada_used, a1_made, a1T_ps, gain_made, hf_made, hhi_made, hlo_made = sems(
        "ada_used a1_made a1T_ps gain_made hf_made hhi_made hlo_made")
    hi_made, lo_made, win_used, pads_set, unit_ps, unit_out, glu_made, conv_made = sems(
        "hi_made lo_made win_used pads_set unit_ps unit_out glu_made conv_made")
    qk_var, qk_rsraw, qk_made, pooled_made, arow_fin, rows_sent = sems(
        "qk_var qk_rsraw qk_made pooled_made arow_fin rows_sent")
    sums_ps, mean_read, csq_made, fpq_ps, fpq_made, lnv_made, ln_raw, ln_app, silu_z, cmix_hi, cmix_lo = sems(
        "sums_ps mean_read csq_made fpq_ps fpq_made lnv_made ln_raw ln_app silu_z cmix_hi cmix_lo")
    pm_ps, pm_hi, pm_lo, fm_ps, fm_hi, fm_lo = sems("pm_ps pm_hi pm_lo fm_ps fm_hi fm_lo")
    khi_made, klo_made, vs_hi, vs_lo, kT_ps, kT_made = sems("khi_made klo_made vs_hi vs_lo kT_ps kT_made")
    qs_hi, qs_lo, qT_ps, qT_made, s_ps, nb_made, p_made, rd_made, diag_made, t_ps, pt_hi, pt_lo = sems(
        "qs_hi qs_lo qT_ps qT_made s_ps nb_made p_made rd_made diag_made t_ps pt_hi pt_lo")
    pv_ps, av_made, am_hi, am_lo, am_chain = sems("pv_ps av_made am_hi am_lo am_chain")
    wo_hi, wo_lo, wo_used, mo_ps, x2_made = sems(
        "wo_hi wo_lo wo_used mo_ps x2_made")
    h2_made, h2T_ps, h2T_made, lgT_ps, lgT_made, lg_ps = sems("h2_made h2T_ps h2T_made lgT_ps lgT_made lg_ps")
    h2_sent = [sem(f"h2_sent{s}") for s in range(2)]
    gsub_made, gexp_made, A_made, rank_ps, slots_made, list_sent, idx_in, np_made, first_lo = sems(
        "gsub_made gexp_made A_made rank_ps slots_made list_sent idx_in np_made first_lo")
    m_in = [sem(f"m_in{n}") for n in range(6)]
    xg_in = [sem(f"xg_in{q}") for q in range(2)]
    y_sent = [sem(f"y_sent{q}") for q in range(2)]
    g_hi, g_lo, u_hi, u_lo, dh_made, dl_made, xt_ps, xt_hi, xt_lo, gu_ps, sg_made, hid_made, ht_ps, ht_hi, ht_lo, dn_ps, ys_a, ys_b, idxc_made = sems(
        "g_hi g_lo u_hi u_lo dh_made dl_made xt_ps xt_hi xt_lo gu_ps sg_made hid_made ht_ps ht_hi ht_lo dn_ps ys_a ys_b idxc_made")
    ya_in = [sem(f"ya_in{t}") for t in range(TT)]
    yo_sent = [sem(f"yo_sent{s}") for s in range(2)]
    ya_scaled, y_made, x3_made, yo_made = sems("ya_scaled y_made x3_made yo_made")

    wa = w_ada[0].rearrange("(k p) n -> p k n", p=P)
    wi = w_in[0].rearrange("(k p) n -> p k n", p=P)
    wo = w_out[0].rearrange("(k p) n -> p k n", p=P)
    w_g = moe_w_gate[0].rearrange("e (k p) n -> p e k n", p=P)
    w_u = moe_w_up[0].rearrange("e (k p) n -> p e k n", p=P)
    w_d = moe_w_down[0].rearrange("e (f p) n -> p e f n", p=P)
    y_slots = y_rows.rearrange("(p s) n -> p s n", s=NTILE)
    A2_FIRST = ADA1 + N_WIN
    WO_FIRST = A2_FIRST + ADA2
    N_WO = 8
    N_ROUND = ADA2 // NRAW

    def raw_count(n):
        return n % NRAW, 16 * (n // NRAW + 1)

    def wait_raw(eng, n):
        s, v = raw_count(n)
        eng.wait_ge(raw_in[s], v)
        return raw[s]

    UNIT_BANK = [2 * (u % 3) for u in range(2 * N_CHAN)] + [0, 1, 2, 3, 4] + [5, 6, 7, 0, 1] + [2, 3, 4, 5, 6]
    N_UNITS = len(UNIT_BANK)
    UNIT_WAIT = [max(u - 2, 0) for u in range(2 * N_CHAN)] + [10, 10, 11, 11, 12] + [12, 12, 12, 13, 14] + [15, 16, 17, 18, 19]

    def mixrow(k):
        return mix1[:, k] if k < 8 else mix2[:, 4 + k - 8] if k < 12 else mix2[:, k - 12]

    def load_weights(eng, e, q, m):
        src = (w_g, w_u, w_d)[m][:, bass.ds(e, 1), :, :].rearrange("p a k n -> p (a k) n")
        eng.dma_start(m_raw[3 * q + m][:, :].rearrange("p (k n) -> p k n", k=KB if m < 2 else 2), src).then_inc(m_in[3 * q + m], 16)

    def parts(nkt):
        return [(0, 2), (2, 5)] if nkt == 5 else [(0, nkt)]

    def part_count(t, nkt, h, i):
        n = len(parts(nkt))
        return t * (2 * HEADS) + (n * h + i + 1)

    def part_ps(i, n):
        return bank(4 + i, 0, n * P).rearrange("p (k s) -> p k s", k=n)

    block = ctx.enter_context(nc.Block())

    @block.sync
    def _(sp):
        def chunk(n, src, k):
            s = n % NRAW
            sp.dma_start(raw[s][:, :].rearrange("p (k n) -> p k n", k=k), src).then_inc(raw_in[s], 16)

        sp.wait_ge(rows_in, 16 * 11)
        for n in range(A2_FIRST + NRAW):
            if n == 2:
                for t in range(TT):
                    sp.dma_start(x[:, t, :], x_sample[0, t * P:(t + 1) * P, :] if t < LT else x_prompt[0]).then_inc(x_in[t], 16)
            if NRAW <= n < ADA1 + NRAW:
                sp.wait_ge(ada_used, n - NRAW + 1)
            elif n >= ADA1 + NRAW:
                sp.wait_ge(lo_made, n - NRAW - ADA1 + 1)
            if n < ADA1:
                chunk(n, wa[:, :, n * CH:(n + 1) * CH], KB)
            elif n < A2_FIRST:
                k, nk, col, cols = W_IN[n - ADA1]
                chunk(n, wi[:, k:k + nk, col:col + cols], nk)
            else:
                a = n - A2_FIRST + ADA1
                chunk(n, wa[:, :, a * CH:(a + 1) * CH], KB)
        sp.wait_ge(unit_ps, N_UNITS)
        sp.dma_start(brow[0:2, :], b_ada[0, 2 * D:6 * D].partition_broadcast(2)).then_inc(arow_in, 16)
        sp.dma_start(frow[0:2, :], norm_ffn[0].partition_broadcast(2)).then_inc(arow_in, 16)
        sp.dma_start(dft[:, :, :], dft_d.rearrange("(t p) n -> p t n", p=P)).then_inc(dft_in, 16)
        sp.dma_start(pool_wt[:, :, :], pool_w[0].rearrange("g c d -> c g d")).then_inc(poolw_in, 16)
        sp.dma_start(ck[:, :], cache_k[0, 0].rearrange("s h d -> s (h d)")).then_inc(cache_in, 16)
        sp.dma_start(cv[:, :], cache_v[0, 0].rearrange("s h d -> s (h d)")).then_inc(cache_in, 16)
        with sp.Fori(1, ADA2 // NRAW) as r:
            for s in range(NRAW):
                sp.wait_ge(ada_used, r * NRAW + (ADA1 - NRAW + s + 1))
                chunk(A2_FIRST + s, wa[:, :, bass.ds(r * (NRAW * CH) + (ADA1 + s) * CH, CH)], KB)
        sp.wait_ge(qk_made, 1)
        sp.dma_start(new_k[0, 0].rearrange("s h d -> s (h d)"), qkv[:, LT, 512:640]).then_inc(out_sent, 16)
        sp.dma_start(new_v[0, 0].rearrange("s h d -> s (h d)"), qkv[:, LT, 640:768]).then_inc(out_sent, 16)
        for i in range(NRAW - 1):
            sp.wait_ge(ada_used, ADA1 + ADA2 - NRAW + i + 1)
            n, cc = i // 4, i % 4
            chunk(WO_FIRST + i, wo[:, 4 * cc:4 * cc + 4, n * 512:(n + 1) * 512], 4)
        sp.wait_ge(arow_fin, 1)
        sp.dma_start(mod_rows, arow[0:2, :]).then_inc(rows_sent, 16)

        sp.wait_ge(rows_sent, 16)
        sp.wait_ge(pv_ps, 2 * TT)
        chunk(WO_FIRST + NRAW - 1, wo[:, 4 * (NRAW - 1):4 * NRAW, 0:512], 4)
        row = mod_rows.rearrange("c (v n) -> c v n", v=4)
        for cnd in range(2):
            sp.dma_start(g1t[:, cnd, :], row[cnd, 0].partition_broadcast(P)).then_inc(g1_in, 16)
        for cnd in range(2):
            sp.dma_start(sh2t[:, cnd, :], row[cnd, 1].partition_broadcast(P)).then_inc(tiles_in, 16)
            sp.dma_start(gain2t[:, cnd, :], row[cnd, 2].partition_broadcast(P)).then_inc(tiles_in, 16)
            sp.dma_start(g2t[:, cnd, :], row[cnd, 3].partition_broadcast(P)).then_inc(tiles_in, 16)
        sp.dma_start(fint[:, :], final_norm.partition_broadcast(P)).then_inc(tiles_in, 16)
        sp.dma_start(wr[:, :, 0:4], router_group_w[0].rearrange("(k p) n -> p k n", p=P)).then_inc(rt_in, 16)
        sp.dma_start(wr[:, :, 4:20], router_expert_w[0].rearrange("(k p) n -> p k n", p=P)).then_inc(rt_in, 16)
        sp.dma_start(rt[:, :], rt_d).then_inc(rt_in, 16)
        sp.dma_start(rbias[:, 0:4], router_group_b[0].partition_broadcast(P)).then_inc(rt_in, 16)
        sp.dma_start(rbias[:, 4:20], router_expert_b[0].partition_broadcast(P)).then_inc(rt_in, 16)
        for i in range(NRAW, N_WO):
            sp.wait_ge(wo_lo, i - NRAW + 1)
            n, cc = i // 4, i % 4
            chunk(WO_FIRST + i, wo[:, 4 * cc:4 * cc + 4, n * 512:(n + 1) * 512], 4)
        for t in range(TT):
            sp.wait_ge(h2_made, t + 1)
            sp.dma_start(h2_rows[t * P:(t + 1) * P, :], h2k[t][:, :]).then_inc(h2_sent[t % 2], 16)
            if t == 0:
                for m in range(3):
                    load_weights(sp, 0, 0, m)
        sp.wait_ge(lgT_ps, TT)
        for s in range(2):
            sp.wait_ge(h2_sent[s], 16 * ((TT - s + 1) // 2))
        for m in range(3):
            load_weights(sp, 1, 1, m)
        sp.wait_ge(first_lo, 1)
        load_weights(sp, 2, 0, 0)
        sp.wait_ge(np_made, 1)
        sp.wait_ge(first_lo, 2)
        last = sp.value_load(npi[0:1, 0:1], min_val=NE // 2 - 1, max_val=(NE + 8) // 2)

        def expert(i):
            return sp.value_load(tile_e[0:1, bass.ds(i, 1)], min_val=0, max_val=NE - 1)

        with sp.Fori(0, last) as r:
            for q in range(2):
                e2, e3 = expert(r * 2 + (q + 2)), expert(r * 2 + (q + 3))
                sp.wait_ge(u_lo, r * 2 + (q + 1))
                load_weights(sp, e2, q, 1)
                sp.wait_ge(g_lo, r * 2 + (q + 2))
                load_weights(sp, e3, 1 - q, 0)
        for s in range(2):
            sp.wait_ge(y_sent[s], last * 16 + 32)
        for t in range(TT):
            sp.wait_ge(yo_made, t + 1)
            sp.dma_start(y_sample[0, t * P:(t + 1) * P, :] if t < LT else y_prompt[0], yo[t % 2][:, :]).then_inc(yo_sent[t % 2], 16)
        for s in range(2):
            sp.wait_ge(yo_sent[s], 16 * ((TT - s + 1) // 2))
        sp.wait_ge(rows_sent, 16)
        sp.wait_ge(list_sent, 160)
        sp.wait_ge(zlist_in, 32)
        sp.wait_ge(out_sent, 32)

    @block.tensor
    def _(pe):
        pe.wait_ge(cst_in, 16)
        pe.wait_ge(rows_in, 16 * 11)
        idc = cst[:, C_ID:C_ID + P]
        pe.transpose(bank(7, 0, N_ROWS), rows1[0:N_ROWS, :], idc[0:N_ROWS, 0:N_ROWS])
        pe.transpose(bank(7, 128, 128 + 4 * TAPS), rows2[0:4 * TAPS, :], idc[0:4 * TAPS, 0:4 * TAPS]).then_inc(rowsT, 1)
        def transposes():
            for k in range(KB):
                if k == 0:
                    pe.wait_ge(xs_made, TT)
                if k >= 3:
                    pe.wait_ge(xn_made, k - 2)
                for t in range(TT):
                    tr = pe.transpose(pair(k % 3)[:, t * P:(t + 1) * P], xs[:, t, k * P:(k + 1) * P], idc)
                tr.then_inc(xT_ps, 1)

        def ada_chunk(w, out):
            for k in range(KB):
                mm = pe.matmul(out[0:2, 0:CH], condT[:, k, :], w[:, k * CH:(k + 1) * CH], start=(k == 0), stop=(k == KB - 1))
            mm.then_inc(ada_used, 1)

        pe.wait_ge(cond_made, 1)
        for n in range(ADA1):
            w = wait_raw(pe, n)
            if n >= 2:
                pe.wait_ge(a1_made, n - 1)
            ada_chunk(w, bank(6 + n % 2))
            if n == ADA1 - 3:
                transposes()
        pe.wait_ge(a1_made, ADA1)
        for b in range(16):
            tr = pe.transpose(bank(6, 2 * b, 2 * b + 2), a1row[0:2, b * P:(b + 1) * P], idc[0:2, 0:2])
        tr.then_inc(a1T_ps, 1)

        def split_mm(out, wh, wl, mh, ml, first, last):
            pe.matmul(out, wh, mh, start=first, stop=False)
            pe.matmul(out, wh, ml, start=False, stop=False)
            return pe.matmul(out, wl, mh, start=False, stop=last)

        unit = 0
        for j, (k0, nk, _, cols) in enumerate(W_IN):
            pe.wait_ge(lo_made, j + 1)
            hi = w_hi[j % 2][:, :].rearrange("p (k n) -> p k n", k=nk)
            lo = w_lo[j % 2][:, :].rearrange("p (k n) -> p k n", k=nk)
            ends = k0 + nk == KB
            for v in range(2 if j < N_CHAN else TT):
                u = unit + v
                if UNIT_WAIT[u] and k0 == 0:
                    pe.wait_ge(unit_out, UNIT_WAIT[u])
                for k in range(nk):
                    first, last = k0 + k == 0, k0 + k == KB - 1
                    if u == 0:
                        pe.wait_ge(hlo_made, k + 1)
                    if j < N_CHAN:
                        out = pair(u % 3)
                        wh, wl = hi[:, k, v * P:(v + 1) * P], lo[:, k, v * P:(v + 1) * P]
                        for a, b in ((0, N_LAT), (N_LAT, TOK)):
                            pe.matmul(out[:, a:b], wh, hT[:, k, 0, a:b], start=first, stop=False)
                            pe.matmul(out[:, a:b], wh, hT[:, k, 1, a:b], start=False, stop=False)
                        for a, b in ((N_LAT, TOK), (0, N_LAT)):
                            mm = pe.matmul(out[:, a:b], wl, hT[:, k, 0, a:b], start=False, stop=last)
                    else:
                        tok = slice(v * P, (v + 1) * P)
                        out = bank(UNIT_BANK[u], 0, cols)
                        mm = split_mm(out, hT[:, k0 + k, 0, tok], hT[:, k0 + k, 1, tok], hi[:, k, :], lo[:, k, :], first, last)
                if ends:
                    mm.then_inc(unit_ps, 1)
            if ends:
                unit += 2 if j < N_CHAN else TT
            else:
                mm.then_inc(win_used, 1)
        pe.wait_ge(unit_out, N_UNITS)
        with pe.Fori(0, ADA2 // NRAW) as r:
            for s in range(NRAW):
                slot, v = raw_count(A2_FIRST + s)
                pe.wait_ge(raw_in[slot], r * 16 + v)
                if s == 0:
                    pe.wait_ge(a1_made, r + ADA1)
                ada_chunk(raw[slot], bank(6 + s // 2, s % 2 * CH, 512))
        pe.wait_ge(ones_set, 1)
        pe.wait_ge(conv_made, 4)

        def over_channels(out, rows):
            for blk in range(4):
                for a, b in ((0, 512), (512, CY)):
                    mm = pe.matmul(out[:, a:b], ones[:, :], rows[:, blk, a:b], start=(blk == 0), stop=(blk == 3))
            return mm

        over_channels(pair(0, CY), cy).then_inc(sums_ps, 1)
        pe.wait_ge(dft_in, 16)
        for n in range(8):
            h, part = n // 2, n % 2
            if n >= 3:
                pe.wait_ge(fpq_made, n - 2)
            if n == 2:
                pe.wait_ge(mean_read, 1)
            out = pair((1 + n) % 3)
            for t in range(LT):
                pe.matmul(out[:, 0:N_LAT], fu[:, t, h * P:(h + 1) * P], dft[:, t, part * 512:(part + 1) * 512], start=(t == 0), stop=(t == LT - 1))
            pe.matmul(out[:, N_LAT:TOK], fu[:, LT, h * P:(h + 1) * P], cst[:, C_DPR + part * P:C_DPR + (part + 1) * P],
                      start=True, stop=True).then_inc(fpq_ps, 1)
        pe.wait_ge(csq_made, 4)
        pe.wait_ge(fpq_made, 6)
        over_channels(pair(0, CY), csq).then_inc(sums_ps, 1)
        for kt in range(6):
            pe.wait_ge(klo_made, kt + 1)
            if kt >= 2:
                pe.wait_ge(kT_made, kt - 1)
            for n in range(4):
                hl, j = n // 2, n % 2
                tr = pe.transpose(bank(6 + kt % 2, n * P, (n + 1) * P), ks[kt % 2][:, hl, j, :, :].rearrange("p a d -> p (a d)").bitcast(f32), ident[:, :])
            tr.then_inc(kT_ps, 1)
        pe.wait_ge(poolw_in, 16)
        pe.wait_ge(pooled_made, 1)
        for g in range(4):
            if g < 2:
                pe.wait_ge(fpq_made, 7 + g)
            elif g == 2:
                pe.wait_ge(lnv_made, 1)
            else:
                pe.wait_ge(pm_lo, g - 2)
            out = pair((1 + g) % 3)
            pe.matmul(out[:, 0:N_LAT], pool_wt[:, g, :], pool_u[:, g, PPAD:PPAD + N_LAT], start=True, stop=True)
            pe.matmul(out[:, N_LAT:TOK], pool_wt[:, g, :], pool_u[:, g, 2 * PPAD + N_LAT:2 * PPAD + TOK], start=True, stop=True).then_inc(pm_ps, 1)
        for h in range(4):
            pe.wait_ge(pm_lo, min(h + 2, 4)) if h < 3 else pe.wait_ge(fm_lo, 1)
            out = pair((2 + h) % 3)
            for a, b in ((0, N_LAT), (N_LAT, TOK)):
                pe.matmul(out[:, a:b], cst[:, C_DCH:C_DCH + P], fpq[:, h, 0, a:b], start=True, stop=False)
                mm = pe.matmul(out[:, a:b], cst[:, C_DCH + P:C_DCH + 2 * P], fpq[:, h, 1, a:b], start=False, stop=True)
            mm.then_inc(fm_ps, 1)
        pe.wait_ge(fm_lo, 4)
        pe.wait_ge(a1_made, ADA1 + N_ROUND)
        pe.wait_ge(kT_made, 6)
        pe.wait_ge(vs_lo, 6)

        def queries(t):
            pe.wait_ge(qs_lo, t + 1)
            for h in range(HEADS):
                tr = pe.transpose(bank(4 + h // 4, (h % 4) * P, (h % 4 + 1) * P), qs[:, h, :, :].rearrange("p a d -> p (a d)").bitcast(f32), ident[:, :])
            tr.then_inc(qT_ps, 1)

        def attend(t, spans, key0, kt0, nkt, more):
            pe.wait_ge(qT_made, t + 1)

            def scores(h):
                if h >= 2:
                    pe.wait_ge(p_made, t * HEADS + (h - 1))
                out = pair(h % 2)
                for hl in range(2):
                    for a, b in spans:
                        mm = pe.matmul(out[:, a:b], qT[:, h, :], kHL[:, hl, h // GRP, key0 + a:key0 + b], start=(hl == 0), stop=(hl == 1))
                mm.then_inc(s_ps, 1)

            scores(0)
            scores(1)
            for h in range(HEADS):
                g = h // GRP
                pe.wait_ge(diag_made, t * HEADS + (h + 1))
                for i, (a, b) in enumerate(parts(nkt)):
                    if h:
                        pe.wait_ge(pt_lo, part_count(t, nkt, h - 1, i))
                    for kt in range(a, b):
                        tr = pe.matmul(bank(4 + i, (kt - a) * P, (kt - a + 1) * P), pb[h % 2][:, kt * P:(kt + 1) * P], diag[h % 2][:, :], start=True, stop=True)
                    tr.then_inc(t_ps, 1)
                if h + 2 < HEADS:
                    scores(h + 2)
                if h % GRP == GRP - 1:
                    pe.wait_ge(pt_lo, part_count(t, nkt, h, len(parts(nkt)) - 1))
                    if more and h == HEADS - 1:
                        queries(t + 1)
                    out = bank(6 + g)
                    for kt in range(nkt):
                        ph = pth[:, kt, :, :].rearrange("p h q -> p (h q)")
                        pl = ptl[:, kt, :, :].rearrange("p h q -> p (h q)")
                        mm = split_mm(out, *(vs[:, kt0 + kt, hl, g, :, :].rearrange("p a d -> p (a d)") for hl in range(2)), ph, pl, kt == 0, kt == nkt - 1)
                    mm.then_inc(pv_ps, 1)

        queries(0)
        with pe.Fori(0, LT) as t:
            attend(t, ((0, 512), (512, 640)), 0, 0, 5, True)
        attend(LT, ((0, P),), 5 * P, 5, 1, False)
        pe.wait_ge(am_lo, 2 * TT)
        for i in range(N_WO):
            n, cc = i // 4, i % 4
            pe.wait_ge(wo_lo, i + 1)
            hi = w_hi[i % 2][:, :].rearrange("p (k n) -> p k n", k=4)
            lo = w_lo[i % 2][:, :].rearrange("p (k n) -> p k n", k=4)
            for t in range(TT):
                if n and cc == 0 and t >= 3:
                    pe.wait_ge(x2_made, t - 2)
                tok = slice(t * P, (t + 1) * P)
                for kk in range(4):
                    m = mixrow(4 * cc + kk)
                    mm = split_mm(bank((5 * n + t) % 8), m[:, 0, tok], m[:, 1, tok], hi[:, kk, :], lo[:, kk, :], i % 4 == 0 and kk == 0, cc == 3 and kk == 3)
                if cc == 3:
                    mm.then_inc(mo_ps, 1)
            if cc < 3:
                mm.then_inc(wo_used, 1)
        pe.wait_ge(rt_in, 80)
        def rows_T(t):
            pe.wait_ge(h2_made, t + 1)
            for k in range(KB):
                tr = pe.transpose(pair(1 + t % 2, D)[:, k * P:(k + 1) * P], h2k[t][:, k * P:(k + 1) * P], ident[:, :])
            tr.then_inc(h2T_ps, 1)

        rows_T(0)
        for t in range(TT):
            if t + 1 < TT:
                if t >= 1:
                    pe.wait_ge(h2T_made, t)
                rows_T(t + 1)
            pe.wait_ge(h2T_made, t + 1)
            if t >= 2:
                pe.wait_ge(lgT_made, t - 1)
            for k in range(KB):
                mm = pe.matmul(bank(6 + t % 2, 0, P)[0:20, :], wr[:, k, :], h2T[t % 2][:, k, :], start=(k == 0), stop=(k == KB - 1))
            mm.then_inc(lgT_ps, 1)
        for t in range(TT):
            pe.wait_ge(lgT_made, t + 1)
            tr = pe.transpose(bank(0, 20 * t, 20 * t + 20), lgT[0:20, t * P:(t + 1) * P], ident[0:20, 0:20])
        tr.then_inc(lg_ps, 1)
        pe.wait_ge(A_made, 1)
        used = AA[:, :, :, :].rearrange("p t g e -> p (t g e)")
        pe.matmul(bank(1, 0, TT * NE), rt[:, R_U:R_U + P], used, start=True, stop=True)
        pe.matmul(bank(1, 128, 128 + TT * NE), ones[:, :], used, start=True, stop=True).then_inc(rank_ps, 1)

        def tokens(r, q):
            pe.wait_ge(xg_in[q], r * 16 + 16)
            for k in range(KB):
                tr = pe.transpose(pair(0, D)[:, k * P:(k + 1) * P], xg[q][:, k * P:(k + 1) * P], ident[:, :])
            tr.then_inc(xt_ps, 1)

        def head(i, r_next, q, more):
            pe.wait_ge(u_lo, i + 1)
            pe.wait_ge(xt_lo, i + 1)
            for k in range(KB):
                mm = split_mm(bank(2 + q), xt_h[q][:, k, :], xt_l[q][:, k, :], gu_hi[q][:, k, :], gu_lo[q][:, k, :], k == 0, k == KB - 1)
            mm.then_inc(gu_ps, 1)
            if more:
                tokens(r_next, 1 - q)
            pe.wait_ge(hid_made, i + 1)
            for f in range(2):
                tr = pe.transpose(bank(4, f * P, (f + 1) * P), hid[:, f * P:(f + 1) * P], ident[:, :])
            tr.then_inc(ht_ps, 1)

        def tail(i, q):
            pe.wait_ge(ht_lo, i + 1)
            pe.wait_ge(dl_made, i + 1)
            pe.wait_ge(ys_a, i + 1)
            pe.wait_ge(ys_b, i + 1)
            for f in range(2):
                for n in range(2):
                    half = slice(n * 512, (n + 1) * 512)
                    mm = split_mm(bank(6 + n), ht_h[q][:, f, :], ht_l[q][:, f, :], d_hi[:, f, half], d_lo[:, f, half], f == 0, f == 1)
            mm.then_inc(dn_ps, 1)

        pe.wait_ge(np_made, 1)
        last = pe.value_load(npi[0:1, 0:1], min_val=NE // 2 - 1, max_val=(NE + 8) // 2)
        tokens(0, 0)
        pe.wait_ge(first_lo, 2)
        head(0, 0, 0, True)
        with pe.Fori(0, last) as r:
            head(r * 2 + 1, r + 1, 1, True)
            tail(r * 2, 0)
            head(r * 2 + 2, r + 1, 0, True)
            tail(r * 2 + 1, 1)
        head(last * 2 + 1, None, 1, False)
        tail(last * 2, 0)
        tail(last * 2 + 1, 1)

    @block.scalar
    def _(act):
        act.dma_start(cst[:, :], cst_d).then_inc(cst_in, 16)
        for row, src in ((ROW_C, c.rearrange("a (r p) -> (a r) p", p=P)),
                         (ROW_C + 8, c_ctx.rearrange("(r p) -> r p", p=P)),
                         (ROW_NMIX, norm_mix.rearrange("a (r p) -> (a r) p", p=P)),
                         (ROW_NFFN, norm_ffn.rearrange("a (r p) -> (a r) p", p=P)),
                         (ROW_FIN, final_norm.rearrange("(r p) -> r p", p=P)),
                         (ROW_BADA, b_ada.rearrange("a (r p) -> (a r) p", p=P)),
                         (ROW_CB, conv_b.rearrange("a (r p) -> (a r) p", p=P)),
                         (ROW_LG, conv_ln_g.rearrange("a (r p) -> (a r) p", p=P)),
                         (ROW_LB, conv_ln_b.rearrange("a (r p) -> (a r) p", p=P)),
                         (ROW_PS, pool_scale.rearrange("a (r p) -> (a r) p", p=P))):
            act.dma_start(rows1[row:row + src.shape[0], :], src).then_inc(rows_in, 16)
        act.dma_start(rows2[0:4 * TAPS, :], conv_w[0].rearrange("w (r p) -> (w r) p", p=P)).then_inc(rows_in, 16)
        act.wait_ge(vec_made, 1)
        act.activation(condT[:, :, :].rearrange("p k c -> p c k"), vec[:, ROW_C:ROW_C + 16].rearrange("p (c k) -> p c k", c=2),
                       ACT.Silu).then_inc(cond_made, 1)
        act.wait_ge(cst_in, 16)
        act.activation(ident[:, :], cst[:, C_ID:C_ID + P], ACT.Copy)
        def ada_row(n):
            act.wait_ge(ada_used, n + 1)
            act.activation(a1row[0:2, n * CH:(n + 1) * CH], bank(6 + n % 2)[0:2, 0:CH], ACT.Copy).then_inc(a1_made, 1)

        for t in range(TT):
            act.wait_ge(x_in[t], 16)
            act.activation(xn[:, :, :].rearrange("p k n -> p (k n)")[:, t * D:(t + 1) * D], x[:, t, :], ACT.Square,
                           accum_out=ss[:, t:t + 1]).then_inc(sq_made, 1)
            if t == 1:
                ada_row(0)
            if t == 3:
                ada_row(1)
        act.wait_ge(var_made, 1)
        act.activation(rs_x[:, 0:TT], var_x[:, 0:TT], ACT.Sqrt).then_inc(rs_raw, 1)
        UNITS_AT = [2, 4, 6, 8, 10, 12, 12, 17, 17, 22, 27]

        def split_hi(j):
            act.wait_ge(raw_in[(ADA1 + j) % NRAW], raw_count(ADA1 + j)[1])
            if j >= 2:
                if W_IN[j - 2][0] + W_IN[j - 2][1] < KB:
                    act.wait_ge(win_used, 1 if j - 2 < 8 else 2)
                else:
                    act.wait_ge(unit_ps, UNITS_AT[j - 2])
            act.activation(w_hi[j % 2][:, :], raw[(ADA1 + j) % NRAW][:, :], ACT.Copy).then_inc(hi_made, 1)

        for n in range(2, ADA1):
            ada_row(n)
            if n == ADA1 - 2:
                split_hi(0)
        act.wait_ge(gain_made, 1)
        for k in range(KB):
            act.wait_ge(xn_made, k + 1)
            if k >= 2:
                act.wait_ge(hlo_made, k - 1)
            for cnd, (a, b) in enumerate(((0, N_LAT), (N_LAT, TOK))):
                act.activation(hf[k % 2][:, a:b], xn[:, k, a:b], ACT.Identity, bias=mods[:, k, cnd:cnd + 1],
                               scale=gain1[:, k, cnd:cnd + 1]).then_inc(hf_made, 1)
            act.wait_ge(hf_made, 2 * k + 2)
            act.activation(hT[:, k, 0, :], hf[k % 2][:, :], ACT.Copy).then_inc(hhi_made, 1)
            if k == 3:
                split_hi(1)
        act.dma_start(rope[:, :, :, :].rearrange("p t a i -> p t (a i)"), rope_d.rearrange("(t p) i -> p t i", p=P)).then_inc(tabs_in, 16)
        for h in range(HEADS + KV):
            src = q_norm if h < HEADS else k_norm
            act.dma_start(qk_gain[:, h * HD:(h + 1) * HD], src[0].partition_broadcast(P)).then_inc(tabs_in, 16)
        act.wait_ge(pads_set, 2)
        unit = 0
        for j, (k0, nk, col, cols) in enumerate(W_IN):
            for v in range((2 if j < N_CHAN else TT) if k0 + nk == KB else 0):
                u = unit + v
                act.wait_ge(unit_ps, u + 1)
                if j < N_CHAN:
                    out = pair(u % 3)
                else:
                    out = bank(UNIT_BANK[u], 0, cols)
                if j in (0, 2):
                    blk = j + v
                    act.activation(cu[:, blk, HALF:HALF + N_LAT], out[:, 0:N_LAT], ACT.Copy)
                    act.activation(cu[:, blk, 2 * HALF + N_LAT:2 * HALF + TOK], out[:, N_LAT:TOK], ACT.Copy).then_inc(unit_out, 1)
                elif j in (1, 3):
                    blk = j - 1 + v
                    if blk >= 2:
                        act.wait_ge(glu_made, blk - 1)
                    act.activation(gate_s[blk % 2][:, :], out, ACT.Sigmoid).then_inc(unit_out, 1)
                elif j in (4, 5):
                    g = 2 * (j - 4) + v
                    act.activation(pool_u[:, g, PPAD:PPAD + N_LAT], out[:, 0:N_LAT], ACT.Copy)
                    act.activation(pool_u[:, g, 2 * PPAD + N_LAT:2 * PPAD + TOK], out[:, N_LAT:TOK], ACT.Copy).then_inc(unit_out, 1)
                elif j in (7, 10):
                    act.activation(qkv[:, v, col:col + cols], out, ACT.Copy).then_inc(unit_out, 1)
                else:
                    act.activation(fu[:, v, :], out, ACT.Copy).then_inc(unit_out, 1)
            if k0 + nk == KB:
                unit += 2 if j < N_CHAN else TT
            if j + 2 < N_WIN:
                split_hi(j + 2)
        def ada_rows(r):
            act.wait_ge(ada_used, ADA1 + (r + 1) * NRAW)
            act.activation(arow[0:2, r * NRAW * CH:(r + 1) * NRAW * CH], pair(3, NRAW * CH)[0:2, :], ACT.Copy).then_inc(a1_made, 1)

        ada_rows(0)
        act.wait_ge(qk_var, 1)
        act.activation(rs_qk[:, :], ss_qk[:, :], ACT.Sqrt).then_inc(qk_rsraw, 1)
        for r in range(1, N_ROUND):
            ada_rows(r)
        act.wait_ge(arow_fin, 1)
        for n in range(8):
            act.wait_ge(fpq_ps, n + 1)
            act.activation(fpq[:, n // 2, n % 2, :], pair((1 + n) % 3), ACT.Copy).then_inc(fpq_made, 1)
            if n == 3:
                for blk in range(4):
                    act.wait_ge(mean_read, blk + 1)
                    act.activation(csq[:, blk, :], cy[:, blk, :], ACT.Square).then_inc(csq_made, 1)
        def keys_out(kt):
            act.wait_ge(kT_ps, kt + 1)
            act.activation(kHL[:, :, :, kt * P:(kt + 1) * P].rearrange("p a j s -> p (a j) s"), bank(6 + kt % 2).rearrange("p (n s) -> p n s", n=4),
                           ACT.Copy).then_inc(kT_made, 1)

        act.wait_ge(qk_made, 5)
        act.wait_ge(cache_in, 32)
        for kt in range(6):
            ksrc = ck[:, :] if kt == 0 else qkv[:, kt - 1, 512:640]
            if kt >= 2:
                act.wait_ge(kT_ps, kt - 1)
            act.activation(ks[kt % 2][:, 0, :, :, :], ksrc.rearrange("p (j d) -> p j d", j=KV).unsqueeze(2).broadcast_to([P, KV, 2, HD]),
                           ACT.Copy).then_inc(khi_made, 1)
            if kt >= 1:
                keys_out(kt - 1)
        keys_out(5)
        act.wait_ge(lnv_made, 1)
        act.activation(ln_r[:, :], ln_v[:, :], ACT.Ln).then_inc(ln_raw, 1)
        act.wait_ge(ln_raw, 1)
        act.activation(ln_r[:, :], ln_r[:, :], ACT.Exp, scale=-0.5).then_inc(ln_raw, 1)
        for blk in range(4):
            act.wait_ge(ln_app, blk + 1)
            if blk == 0:
                act.wait_ge(rows_sent, 16)
            if blk >= 2:
                act.wait_ge(cmix_lo, blk - 1)
            for a, b, o in ((0, N_LAT, 0), (N_LAT, TOK, HALF)):
                act.activation(gate_s[blk % 2][:, a:b], cy[:, blk, a + o:b + o], ACT.Silu, bias=vec[:, ROW_LB + blk:ROW_LB + blk + 1],
                               scale=vec[:, ROW_LG + blk:ROW_LG + blk + 1]).then_inc(silu_z, 1)
            act.wait_ge(silu_z, 2 * blk + 2)
            act.activation(mix1[:, 4 + blk, 0, :], gate_s[blk % 2][:, :], ACT.Copy).then_inc(cmix_hi, 1)
        act.wait_ge(cmix_lo, 4)
        for g in range(4):
            act.wait_ge(pm_ps, g + 1)
            act.activation(mix2[:, 4 + g, 0, :], pair((1 + g) % 3), ACT.Copy, scale=vec[:, ROW_PS + g:ROW_PS + g + 1]).then_inc(pm_hi, 1)
        for h in range(4):
            act.wait_ge(fm_ps, h + 1)
            act.activation(mix2[:, h, 0, :], pair((2 + h) % 3), ACT.Copy).then_inc(fm_hi, 1)
        act.wait_ge(qk_made, 5)
        act.wait_ge(fm_ps, 4)
        for kt in range(6):
            vsrc = cv[:, :] if kt == 0 else qkv[:, kt - 1, 640:768]
            act.activation(vs[:, kt, 0, :, :, :], vsrc.rearrange("p (j d) -> p j d", j=KV).unsqueeze(2).broadcast_to([P, KV, 2, HD]),
                           ACT.Copy).then_inc(vs_hi, 1)

        def queries_hi(t):
            act.activation(qs[:, :, 0, :], qkv[:, bass.ds(t, 1), 0:512].rearrange("p a (h d) -> p (a h) d", h=HEADS), ACT.Copy).then_inc(qs_hi, 1)

        def queries_out(t):
            act.wait_ge(qT_ps, t + 1)
            act.activation(qT[:, :, :].rearrange("p h q -> p (h q)"), pair(2, 1024), ACT.Copy).then_inc(qT_made, 1)

        def attend(t, w, nkt, more):
            def probs(h):
                act.wait_ge(nb_made, t * HEADS + (h + 1))
                if h >= 2:
                    act.wait_ge(t_ps, part_count(t, nkt, h - 2, len(parts(nkt)) - 1))
                act.activation(pb[h % 2][:, 0:w], pair(h % 2)[:, 0:w], ACT.Exp, bias=nbias[:, h:h + 1], scale=HD ** -0.5,
                               accum_out=den[:, h:h + 1]).then_inc(p_made, 1)

            probs(0)
            probs(1)
            for h in range(HEADS):
                g = h // GRP
                for i, (a, b) in enumerate(parts(nkt)):
                    act.wait_ge(t_ps, part_count(t, nkt, h, i))
                    if h == GRP:
                        act.wait_ge(pv_ps, t * 2 + 1)
                    act.activation(pth[:, a:b, h % GRP, :], part_ps(i, b - a), ACT.Copy).then_inc(pt_hi, 1)
                if h + 2 < HEADS:
                    probs(h + 2)
                if more and h == HEADS - 3:
                    queries_hi(t + 1)
                if more and h == HEADS - 1:
                    queries_out(t + 1)
                if h % GRP == GRP - 1:
                    act.wait_ge(pv_ps, t * 2 + (g + 1))
                    v = bank(6 + g).rearrange("p (b o q) -> p b o q", b=2, o=2)
                    for o in range(2):
                        act.activation(ctxv[g][64 * o:64 * o + 64, :, :], v[64 * o:64 * o + 64, :, o, :], ACT.Copy).then_inc(av_made, 1)

        act.wait_ge(zlist_in, 32)
        queries_hi(0)
        queries_out(0)
        with act.Fori(0, LT) as t:
            attend(t, 640, 5, True)
        attend(LT, P, 1, False)

        def wo_split(i):
            act.wait_ge(raw_in[(WO_FIRST + i) % NRAW], raw_count(WO_FIRST + i)[1])
            if i == 0:
                act.wait_ge(pv_ps, 2 * TT)
            if i >= 2:
                j = i - 2
                if j % 4 < 3:
                    act.wait_ge(wo_used, 3 * (j // 4) + j % 4 + 1)
                else:
                    act.wait_ge(mo_ps, TT * (j // 4 + 1))
            act.activation(w_hi[i % 2][:, :], raw[(WO_FIRST + i) % NRAW][:, :], ACT.Copy).then_inc(wo_hi, 1)

        for i in range(N_WO):
            wo_split(i)
        act.wait_ge(mo_ps, 2 * TT)
        for t in range(TT):
            act.wait_ge(x2_made, TT + t + 1)
            if t >= 2:
                act.wait_ge(sq_made, TT + t - 1)
            act.activation(sq_out[t % 2][:, :], x[:, t, :], ACT.Square, accum_out=ss[:, t:t + 1]).then_inc(sq_made, 1)
        act.wait_ge(var_made, 2)
        act.activation(rs_x[:, 0:TT], var_x[:, 0:TT], ACT.Sqrt).then_inc(rs_raw, 1)

        def gate_up_hi(q, count, u):
            act.wait_ge(m_in[3 * q + u], count)
            act.activation(gu_hi[q][:, :, u * FF:(u + 1) * FF], m_raw[3 * q + u][:, :].rearrange("p (k n) -> p k n", k=KB),
                           ACT.Copy).then_inc((g_hi, u_hi)[u], 1)

        def down_hi(q, count):
            act.wait_ge(m_in[3 * q + 2], count)
            act.activation(d_hi[:, :, :].rearrange("p f n -> p (f n)"), m_raw[3 * q + 2][:, :], ACT.Copy).then_inc(dh_made, 1)

        def logits_out(t):
            act.wait_ge(lgT_ps, t + 1)
            act.activation(lgT[0:20, t * P:(t + 1) * P], bank(6 + t % 2, 0, P)[0:20, :], ACT.Copy).then_inc(lgT_made, 1)

        for t in range(TT):
            act.wait_ge(h2T_ps, t + 1)
            if t >= 2:
                act.wait_ge(lgT_ps, t - 1)
            act.activation(h2T[t % 2][:, :, :].rearrange("p k n -> p (k n)"), pair(1 + t % 2, D), ACT.Copy).then_inc(h2T_made, 1)
            if t >= 1:
                logits_out(t - 1)
        logits_out(TT - 1)
        gate_up_hi(0, 16, 0)
        gate_up_hi(0, 16, 1)
        down_hi(0, 16)
        act.wait_ge(gsub_made, 1)
        act.activation(ge4[:, :, :], ge4[:, :, :], ACT.Exp).then_inc(gexp_made, 1)
        act.wait_ge(gsub_made, 2)
        act.activation(pe2[:, :], pe2[:, :], ACT.Exp).then_inc(gexp_made, 1)
        gate_up_hi(1, 16, 0)
        gate_up_hi(1, 16, 1)

        def tokens_hi(n, q):
            act.wait_ge(xt_ps, n + 1)
            act.activation(xt_h[q][:, :, :].rearrange("p k n -> p (k n)"), pair(0, D), ACT.Copy).then_inc(xt_hi, 1)

        def head(i, q, more):
            act.wait_ge(gu_ps, i + 1)
            act.activation(sg[:, :], bank(2 + q, 0, FF), ACT.Silu).then_inc(sg_made, 1)
            if more:
                tokens_hi(i + 1, 1 - q)
            act.wait_ge(ht_ps, i + 1)
            act.activation(ht_h[q][:, :, :].rearrange("p f n -> p (f n)"), bank(4, 0, FF), ACT.Copy).then_inc(ht_hi, 1)

        def tail(i, r, q, next_down):
            act.wait_ge(dn_ps, i + 1)
            act.wait_ge(y_sent[q], r * 16 + 16)
            act.activation(ys[q][:, 0:512], bank(6), ACT.Copy).then_inc(ys_a, 1)
            if next_down:
                down_hi(1 - q, r * 16 + 16 + 16 * q)
            act.wait_ge(ys_a, i + 2)
            act.wait_ge(ys_b, i + 2)
            act.dma_start(y_slots[:, bass.ds(i, 1), :].rearrange("p a n -> p (a n)"), ys[q][:, :]).then_inc(y_sent[q], 16)

        act.wait_ge(np_made, 1)
        last = act.value_load(npi[0:1, 0:1], min_val=NE // 2 - 1, max_val=(NE + 8) // 2)
        tokens_hi(0, 0)
        head(0, 0, True)
        gate_up_hi(0, 32, 0)
        with act.Fori(0, last) as r:
            for q in range(2):
                e2 = act.value_load(tile_e[0:1, bass.ds(r * 2 + (q + 2), 1)], min_val=0, max_val=NE - 1)
                gate_up_hi(q, r * 16 + 32, 1)
                head(r * 2 + (q + 1), 1 - q, True)
                act.wait_ge(dl_made, r * 2 + (q + 1))
                load_weights(act, e2, q, 2)
                gate_up_hi(1 - q, r * 16 + 32 + 16 * q, 0)
                tail(r * 2 + q, r, q, True)
        head(last * 2 + 1, 1, False)
        tail(last * 2, last, 0, True)
        tail(last * 2 + 1, last, 1, False)

        def scale_first(t):
            act.wait_ge(ya_in[t], 32)
            act.activation(ya[t][:, :], ya[t][:, :], ACT.Copy, scale=gates[:, 0, t:t + 1]).then_inc(ya_scaled, 1)

        scale_first(0)
        scale_first(1)
        for t in range(TT):
            if t + 2 < TT:
                scale_first(t + 2)
            act.wait_ge(x3_made, t + 1)
            if t >= 2:
                act.wait_ge(sq_made, 2 * TT + t - 1)
            act.activation(ysq[t % 2][:, :], x[:, t, :], ACT.Square, accum_out=ss[:, t:t + 1]).then_inc(sq_made, 1)
            act.wait_ge(var_made, 3 + t)
            act.activation(rs_x[:, t:t + 1], var_x[:, t:t + 1], ACT.Sqrt).then_inc(rs_raw, 1)

    @block.gpsimd
    def _(pool):
        def link(ins, n=[0]):
            ins.then_inc(pool_chain, 1)
            n[0] += 1
            pool.wait_ge(pool_chain, n[0])

        for n, (s, v) in enumerate(((y_sent[0], 16), (y_sent[1], 16), (ys_a, 1), (ys_b, 1), (g_lo, 1), (u_lo, 1))):
            pool.memset(ahead[:, n:n + 1], 0).then_inc(s, v)
        pool.memset(ones[:, :], 1.0).then_inc(ones_set, 1)
        link(pool.memset(zero_i[:, :], 0))
        pool.dma_start(slot_list.rearrange("(p s) a -> p (s a)", p=P), zero_i[:, :]).then_inc(zlist_in, 16)

        def split_lo(j):
            pool.wait_ge(hi_made, j + 1)
            pool.tensor_tensor(w_lo[j % 2][:, :], raw[(ADA1 + j) % NRAW][:, :], w_hi[j % 2][:, :].bitcast(f32), SUB).then_inc(lo_made, 1)

        split_lo(0)
        pool.wait_ge(hlo_made, KB)
        pool.memset(cu[:, :, :], 0.0).then_inc(pads_set, 1)
        pool.memset(pool_u[:, :, :], 0.0).then_inc(pads_set, 1)
        for j in range(1, N_WIN):
            split_lo(j)
        for g, w in enumerate(WINDOWS):
            pool.wait_ge(unit_out, 8 + g + 1)
            src, have, a, b, s = pool_u[:, g, :], 1, 0, PU, 0
            while have < w:
                dst = pool_t[s][:, :]
                if have == 1:
                    a, b = 1, PU
                    link(pool.tensor_tensor(dst[:, a:b], src[:, a - 1:b - 1], src[:, a:b], ADD))
                else:
                    h = have // 2
                    a, b = a + h, b - h
                    link(pool.tensor_tensor(dst[:, a:b], src[:, a - h:b - h], src[:, a + h:b + h], ADD))
                src, have, s = dst, have * 2, 1 - s
            assert a <= PPAD and b >= PU - PPAD
            for q, (e, left) in enumerate(((PPAD, True), (PPAD + N_LAT, False), (2 * PPAD + N_LAT, True), (2 * PPAD + TOK, False))):
                n = w // 2
                e0 = e if left else e - n
                col = C_EDGE + (g * 4 + q) * 8
                link(pool.tensor_tensor(src[:, e0:e0 + n], src[:, e0:e0 + n], cst[:, col:col + n], MUL))
            mid = slice(PPAD, PU - PPAD)
            link(pool.tensor_scalar(src[:, mid], src[:, mid], 1.0 / w, None, MUL))
            ins = pool.tensor_tensor(pool_u[:, g, mid], src[:, mid], pool_u[:, g, mid], SUB)
            if g < 3:
                link(ins)
        ins.then_inc(pooled_made, 1)
        pool.wait_ge(ada_used, ADA1 + ADA2)
        link(pool.memset(zeros[:, :], 0.0))
        pool.dma_start(y_slots[:, NE:NTILE, :], zeros[:, :].unsqueeze(1).broadcast_to([P, N_OV, D])).then_inc(zlist_in, 16)

        pool.wait_ge(am_lo, 2 * TT)
        for i in range(N_WO):
            pool.wait_ge(wo_hi, i + 1)
            pool.tensor_tensor(w_lo[i % 2][:, :], raw[(WO_FIRST + i) % NRAW][:, :], w_hi[i % 2][:, :].bitcast(f32), SUB).then_inc(wo_lo, 1)
        def gate_up_lo(q, n, u):
            pool.wait_ge((g_hi, u_hi)[u], n + 1)
            cols = slice(u * FF, (u + 1) * FF)
            pool.tensor_tensor(gu_lo[q][:, :, cols], m_raw[3 * q + u][:, :].rearrange("p (k n) -> p k n", k=KB),
                               gu_hi[q][:, :, cols].bitcast(f32), SUB).then_inc(first_lo, 1)

        def down_lo(q):
            pool.tensor_tensor(d_lo[:, :, :].rearrange("p f n -> p (f n)"), m_raw[3 * q + 2][:, :],
                               d_hi[:, :, :].rearrange("p f n -> p (f n)").bitcast(f32), SUB).then_inc(dl_made, 1)

        def gather(q):
            pool.indirect_dma_start(xg[q][:, :], None, h2_rows, bass.IndirectOffsetOnAxis(ap=idxc[q][:, 0:1], axis=0)).then_inc(xg_in[q], 16)

        gate_up_lo(0, 0, 0)
        gate_up_lo(0, 0, 1)
        pool.wait_ge(rt_in, 80)
        link(pool.tensor_copy(tid[:, :], rt[:, R_TID:R_TID + TT]))
        pool.wait_ge(zlist_in, 16)
        pool.wait_ge(slots_made, 1)
        for a in range(2):
            for t in range(TT):
                pool.indirect_dma_start(slot_list, bass.IndirectOffsetOnAxis(ap=slots[:, a, t:t + 1], axis=0), tid[:, t:t + 1], None).then_inc(list_sent, 16)
        pool.wait_ge(list_sent, 160)
        pool.dma_start(idx[:, :], slot_list.rearrange("(p s) a -> p (s a)", p=P)).then_inc(idx_in, 16)
        pool.wait_ge(idx_in, 16)
        for s in range(2):
            pool.wait_ge(h2_sent[s], 16 * ((TT - s + 1) // 2))
        for q in range(2):
            pool.tensor_copy(idxc[q][:, :], idx[:, q:q + 1]).then_inc(idxc_made, 1)
            pool.wait_ge(idxc_made, q + 1)
            gather(q)
        pool.wait_ge(np_made, 1)
        last = pool.value_load(npi[0:1, 0:1], min_val=NE // 2 - 1, max_val=(NE + 8) // 2)

        def look_up(i, q):
            pool.wait_ge(xt_ps, i - 1)
            pool.tensor_tensor(ahead[:, 6:7], zero_i[:, 0:1], zero_i[:, 0:1], ADD)
            pool.tensor_copy(idxc[q][:, :], idx[:, bass.ds(i, 1)]).then_inc(idxc_made, 1)
            pool.wait_ge(idxc_made, i + 1)
            pool.tensor_tensor(ahead[:, 7:8], zero_i[:, 0:1], zero_i[:, 0:1], ADD)
            gather(q)

        with pool.Fori(0, last) as r:
            for q in range(2):
                look_up(r * 2 + (q + 2), q)
                pool.wait_ge(dh_made, r * 2 + (q + 1))
                down_lo(q)
        for q in range(2):
            pool.wait_ge(dh_made, last * 2 + (q + 1))
            down_lo(q)
        for s in range(2):
            pool.wait_ge(y_sent[s], last * 16 + 32)
        pool.tensor_tensor(idxc[0][:, :], idx[:, 0:1], idx[:, 0:1], ADD).then_inc(idxc_made, 1)
        for t in range(TT):
            for a, y in ((0, ya), (1, yb)):
                pool.indirect_dma_start(y[t][:, :], None, y_rows, bass.IndirectOffsetOnAxis(ap=slots[:, a, t:t + 1], axis=0)).then_inc(ya_in[t], 16)
        for t in range(TT):
            pool.wait_ge(y_made, t + 1)
            pool.tensor_tensor(x[:, t, :], x[:, t, :], ya[t][:, :], ADD).then_inc(x3_made, 1)

    @block.vector
    def _(dve):
        def link(ins, n=[0]):
            ins.then_inc(dve_chain, 1)
            n[0] += 1
            dve.wait_ge(dve_chain, n[0])

        def newton(y, v, tmp):
            link(dve.tensor_tensor(tmp, y, y, MUL))
            link(dve.tensor_tensor(tmp, tmp, v, MUL))
            link(dve.tensor_scalar(tmp, tmp, -0.5, 1.5, MUL, ADD))
            link(dve.tensor_tensor(y, y, tmp, MUL))

        def refine(y, v, tmp):
            link(dve.reciprocal(y, y))
            newton(y, v, tmp)

        dve.wait_ge(rowsT, 1)
        link(dve.tensor_copy(vec[:, :], bank(7, 0, N_ROWS)))
        dve.tensor_copy(tapw[:, :], bank(7, 128, 128 + 4 * TAPS)).then_inc(vec_made, 1)
        dve.wait_ge(sq_made, TT)
        dve.tensor_scalar(var_x[:, 0:TT], ss[:, 0:TT], 1.0 / D, EPS, MUL, ADD).then_inc(var_made, 1)
        dve.wait_ge(rs_raw, 1)
        refine(rs_x[:, 0:TT], var_x[:, 0:TT], nw[:, 0:TT])
        for t in range(TT):
            dve.tensor_scalar(xs[:, t, :], x[:, t, :], rs_x[:, t:t + 1], None, MUL).then_inc(xs_made, 1)
        for k in range(KB):
            dve.wait_ge(xT_ps, k + 1)
            dve.tensor_copy(xn[:, k, :], pair(k % 3)).then_inc(xn_made, 1)
        dve.wait_ge(a1T_ps, 1)
        link(dve.tensor_tensor(mods[:, :, :], bank(6, 0, 32).rearrange("p (b c) -> p b c", c=2),
                               vec[:, ROW_BADA:ROW_BADA + 16].unsqueeze(2).broadcast_to([P, 16, 2]), ADD))
        dve.scalar_tensor_tensor(out=gain1[:, :, :], in0=mods[:, 8:16, :], scalar=1.0,
                                 in1=vec[:, ROW_NMIX:ROW_NMIX + 8].unsqueeze(2).broadcast_to([P, 8, 2]), op0=ADD, op1=MUL).then_inc(gain_made, 1)
        for k in range(KB):
            dve.wait_ge(hhi_made, k + 1)
            dve.tensor_tensor(hT[:, k, 1, :], hf[k % 2][:, :], hT[:, k, 0, :].bitcast(f32), SUB).then_inc(hlo_made, 1)

        def glu(blk):
            dve.wait_ge(unit_out, 4 * (blk // 2) + 2 + blk % 2 + 1)
            link(dve.tensor_tensor(cu[:, blk, HALF:HALF + N_LAT], cu[:, blk, HALF:HALF + N_LAT], gate_s[blk % 2][:, 0:N_LAT], MUL))
            dve.tensor_tensor(cu[:, blk, 2 * HALF + N_LAT:2 * HALF + TOK], cu[:, blk, 2 * HALF + N_LAT:2 * HALF + TOK],
                              gate_s[blk % 2][:, N_LAT:TOK], MUL).then_inc(glu_made, 1)

        def conv(blk):
            dve.wait_ge(glu_made, blk + 1)
            link(dve.tensor_scalar(cy[:, blk, :], cu[:, blk, 0:CY], tapw[:, blk:blk + 1], vec[:, ROW_CB + blk:ROW_CB + blk + 1], MUL, ADD))
            for i in range(1, TAPS):
                ins = dve.scalar_tensor_tensor(out=cy[:, blk, :], in0=cu[:, blk, i:i + CY], scalar=tapw[:, 4 * i + blk:4 * i + blk + 1],
                                               in1=cy[:, blk, :], op0=MUL, op1=ADD)
                if i < TAPS - 1:
                    link(ins)
            ins.then_inc(conv_made, 1)

        glu(0)
        glu(1)
        conv(0)
        glu(2)
        glu(3)
        conv(1)
        conv(2)
        conv(3)
        dve.wait_ge(unit_out, N_UNITS)
        for t in range(TT):
            link(dve.tensor_tensor(qtmp[:, :], qkv[:, t, 0:640], qkv[:, t, 0:640], MUL))
            link(dve.tensor_reduce(ss_qk[:, 10 * t:10 * t + 10], qtmp[:, :].rearrange("p (h d) -> p h d", d=HD), AX.X, ADD))
        dve.tensor_scalar(ss_qk[:, :], ss_qk[:, :], 1.0 / HD, EPS, MUL, ADD).then_inc(qk_var, 1)
        dve.wait_ge(tabs_in, 16 * 11)
        dve.wait_ge(qk_rsraw, 1)
        refine(rs_qk[:, :], ss_qk[:, :], nw[:, 0:50])
        for t in (LT, 0, 1, 2, 3):
            heads = qkv[:, t, 0:640].rearrange("p (h d) -> p h d", d=HD)
            link(dve.tensor_tensor(heads, heads, rs_qk[:, 10 * t:10 * t + 10].unsqueeze(2).broadcast_to([P, 10, HD]), MUL))
            ins = dve.tensor_tensor(qkv[:, t, 0:640], qkv[:, t, 0:640], qk_gain[:, :], MUL)
            if t == LT:
                ins.then_inc(qk_made, 1)
                continue
            link(ins)
            two = qkv[:, t, 0:640].rearrange("p (h i a) -> p a h i", h=10, a=2)
            x0, x1 = two[:, 0], two[:, 1]
            cos = rope[:, t, 0:1, :].broadcast_to([P, 10, HD // 2])
            sin = rope[:, t, 1:2, :].broadcast_to([P, 10, HD // 2])
            tv = qtmp[:, :].rearrange("p (a h i) -> p a h i", a=2, h=10)
            zv = rtmp[:, :].rearrange("p (a h i) -> p a h i", a=2, h=10)
            if t:
                dve.wait_ge(qk_made, 1 + t)
            dve.tensor_tensor(tv[:, 0], x0, cos, MUL)
            dve.tensor_tensor(tv[:, 1], x1, sin, MUL)
            dve.tensor_tensor(zv[:, 0], x0, sin, MUL)
            link(dve.tensor_tensor(zv[:, 1], x1, cos, MUL))
            link(dve.tensor_tensor(x0, tv[:, 0], tv[:, 1], SUB))
            dve.tensor_tensor(x1, zv[:, 0], zv[:, 1], ADD).then_inc(qk_made, 1)
        dve.wait_ge(arow_in, 32)
        for r in range(N_ROUND):
            cols = slice(r * NRAW * CH, (r + 1) * NRAW * CH)
            dve.wait_ge(a1_made, ADA1 + r + 1)
            link(dve.tensor_tensor(arow[0:2, cols], arow[0:2, cols], brow[0:2, cols], ADD))
        dve.scalar_tensor_tensor(out=arow[0:2, 2 * D:3 * D], in0=arow[0:2, 2 * D:3 * D], scalar=1.0, in1=frow[0:2, :], op0=ADD, op1=MUL).then_inc(arow_fin, 1)
        dve.wait_ge(pooled_made, 1)
        dve.wait_ge(sums_ps, 1)
        link(dve.tensor_scalar(ln_v[:, :], pair(0, CY), -1.0 / 512, None, MUL))
        for blk in range(4):
            dve.tensor_tensor(cy[:, blk, :], cy[:, blk, :], ln_v[:, :], ADD).then_inc(mean_read, 1)
        for kt in range(6):
            k2 = (ck[:, :] if kt == 0 else qkv[:, kt - 1, 512:640]).rearrange("p (j d) -> p j d", j=KV)
            dve.wait_ge(khi_made, kt + 1)
            if kt >= 2:
                dve.wait_ge(kT_ps, kt - 1)
            for j in range(KV):
                ins = dve.tensor_tensor(ks[kt % 2][:, 1, j, :, :], k2[:, j:j + 1, :].broadcast_to([P, 2, HD]),
                                        ks[kt % 2][:, 0, j, :, :].bitcast(f32), SUB)
            ins.then_inc(klo_made, 1)
        dve.wait_ge(sums_ps, 2)
        dve.wait_ge(mean_read, 4)
        dve.tensor_scalar(ln_v[:, :], pair(0, CY), 1.0 / 512, EPS, MUL, ADD).then_inc(lnv_made, 1)
        dve.wait_ge(lnv_made, 1)
        dve.wait_ge(ln_raw, 2)
        newton(ln_r[:, :], ln_v[:, :], csq[:, 0, :])
        for blk in range(4):
            dve.tensor_tensor(cy[:, blk, :], cy[:, blk, :], ln_r[:, :], MUL).then_inc(ln_app, 1)
        for blk in range(4):
            dve.wait_ge(cmix_hi, blk + 1)
            dve.tensor_tensor(mix1[:, 4 + blk, 1, :], gate_s[blk % 2][:, :], mix1[:, 4 + blk, 0, :].bitcast(f32), SUB).then_inc(cmix_lo, 1)
        for g in range(4):
            dve.wait_ge(pm_hi, g + 1)
            dve.scalar_tensor_tensor(out=mix2[:, 4 + g, 1, :], in0=pair((1 + g) % 3), scalar=vec[:, ROW_PS + g:ROW_PS + g + 1],
                                     in1=mix2[:, 4 + g, 0, :].bitcast(f32), op0=MUL, op1=SUB).then_inc(pm_lo, 1)
        for h in range(4):
            dve.wait_ge(fm_hi, h + 1)
            dve.tensor_tensor(mix2[:, h, 1, :], pair((2 + h) % 3), mix2[:, h, 0, :].bitcast(f32), SUB).then_inc(fm_lo, 1)
        for kt in range(6):
            vsrc = cv[:, :] if kt == 0 else qkv[:, kt - 1, 640:768]
            v2 = vsrc.rearrange("p (j d) -> p j d", j=KV)
            dve.wait_ge(vs_hi, kt + 1)
            for j in range(KV):
                ins = dve.tensor_tensor(vs[:, kt, 1, j, :, :], v2[:, j:j + 1, :].broadcast_to([P, 2, HD]), vs[:, kt, 0, j, :, :].bitcast(f32), SUB)
            ins.then_inc(vs_lo, 1)

        def queries_lo(t):
            dve.wait_ge(qs_hi, t + 1)
            dve.tensor_tensor(qs[:, :, 1, :], qkv[:, bass.ds(t, 1), 0:512].rearrange("p a (h d) -> p (a h) d", h=HEADS),
                              qs[:, :, 0, :].bitcast(f32), SUB).then_inc(qs_lo, 1)

        def attend(t, w, nkt, more):
            def bias(h):
                dve.wait_ge(s_ps, t * HEADS + (h + 1))
                dve.tensor_reduce(smax[:, h:h + 1], pair(h % 2)[:, 0:w], AX.X, ALU.max).then_inc(am_chain, 1)
                dve.wait_ge(am_chain, t * HEADS + (h + 1))
                dve.tensor_scalar(nbias[:, h:h + 1], smax[:, h:h + 1], -(HD ** -0.5), None, MUL).then_inc(nb_made, 1)

            def scale_diag(h):
                dve.wait_ge(p_made, t * HEADS + (h + 1))
                dve.reciprocal(rden[:, h:h + 1], den[:, h:h + 1]).then_inc(rd_made, 1)
                dve.wait_ge(rd_made, t * HEADS + (h + 1))
                if h >= 2:
                    dve.wait_ge(t_ps, part_count(t, nkt, h - 2, len(parts(nkt)) - 1))
                dve.tensor_scalar(diag[h % 2][:, :], ident[:, :], rden[:, h:h + 1], None, MUL).then_inc(diag_made, 1)

            bias(0)
            bias(1)
            scale_diag(0)
            for h in range(HEADS):
                g = h // GRP
                if h + 1 < HEADS:
                    scale_diag(h + 1)
                for i, (a, b) in enumerate(parts(nkt)):
                    dve.wait_ge(pt_hi, part_count(t, nkt, h, i))
                    dve.tensor_tensor(ptl[:, a:b, h % GRP, :], part_ps(i, b - a), pth[:, a:b, h % GRP, :].bitcast(f32), SUB).then_inc(pt_lo, 1)
                if h + 2 < HEADS:
                    bias(h + 2)
                if more and h == HEADS - 2:
                    queries_lo(t + 1)
                if h % GRP == GRP - 1:
                    cols = bass.ds(t * P, P)
                    hi, lo = (mix1[:, 2 * g:2 * g + 2, hl, cols] for hl in range(2))
                    dve.wait_ge(av_made, t * 4 + (2 * g + 2))
                    dve.tensor_scalar(hi, ctxv[g][:, :, :], 1.0, None, MUL).then_inc(am_hi, 1)
                    dve.wait_ge(am_hi, t * 2 + (g + 1))
                    dve.tensor_tensor(lo, ctxv[g][:, :, :], hi.bitcast(f32), SUB).then_inc(am_lo, 1)

        queries_lo(0)
        with dve.Fori(0, LT) as t:
            attend(t, 640, 5, True)
        attend(LT, P, 1, False)
        dve.wait_ge(g1_in, 32)
        for n in range(2):
            for t in range(TT):
                dve.wait_ge(mo_ps, TT * n + t + 1)
                half = slice(n * 512, (n + 1) * 512)
                b = bank((5 * n + t) % 8)
                link(dve.tensor_tensor(b, b, g1t[:, 0 if t < LT else 1, half], MUL))
                dve.tensor_tensor(x[:, t, half], x[:, t, half], b, ADD).then_inc(x2_made, 1)
        dve.wait_ge(sq_made, 2 * TT)
        dve.tensor_scalar(var_x[:, 0:TT], ss[:, 0:TT], 1.0 / D, EPS, MUL, ADD).then_inc(var_made, 1)
        dve.wait_ge(rs_raw, 2)
        refine(rs_x[:, 0:TT], var_x[:, 0:TT], nw[:, 0:TT])
        dve.wait_ge(tiles_in, 7 * 16)
        for t in range(TT):
            cnd = 0 if t < LT else 1
            link(dve.scalar_tensor_tensor(out=h2k[t][:, :], in0=x[:, t, :], scalar=rs_x[:, t:t + 1], in1=gain2t[:, cnd, :], op0=MUL, op1=MUL))
            dve.tensor_tensor(h2k[t][:, :], h2k[t][:, :], sh2t[:, cnd, :], ADD).then_inc(h2_made, 1)

        def first_of(dst, flags):
            link(dve.tensor_copy(seen[:, :, :], flags[:, :, 0:1]))
            dve.tensor_copy(dst[:, :, 0:1], flags[:, :, 0:1])
            for j in range(1, 4):
                link(dve.tensor_tensor(dst[:, :, j:j + 1], flags[:, :, j:j + 1], seen[:, :, :], ALU.is_gt))
                if j < 3:
                    link(dve.tensor_tensor(seen[:, :, :], seen[:, :, :], flags[:, :, j:j + 1], ALU.max))

        def wide(v, n=4):
            return v[:, :].unsqueeze(2).broadcast_to([P, TT, n])

        dve.wait_ge(rt_in, 80)
        dve.wait_ge(lg_ps, 1)
        link(dve.tensor_tensor(lg[:, :, :], bank(0, 0, TT * 20).rearrange("p (t n) -> p t n", t=TT),
                               rbias[:, :].unsqueeze(1).broadcast_to([P, TT, 20]), ADD))
        gl, el = lg[:, :, 0:4], lg[:, :, 4:20].rearrange("p t (g e) -> p t g e", g=NG)
        link(dve.tensor_reduce(gm[:, :], gl, AX.X, ALU.max))
        dve.tensor_tensor(ge4[:, :, :], gl, wide(gm), SUB).then_inc(gsub_made, 1)
        link(dve.tensor_tensor(eq[:, :, :], gl, wide(gm), ALU.is_equal))
        first_of(oh, eq)
        link(dve.tensor_tensor(eg[:, :, :, :], el, oh[:, :, :].unsqueeze(3).broadcast_to([P, TT, NG, EPG]), MUL))
        link(dve.tensor_reduce(e_in[:, :, :], eg[:, :, :, :].rearrange("p t g e -> p t e g"), AX.X, ADD))
        link(dve.tensor_reduce(m1[:, :], e_in[:, :, :], AX.X, ALU.max))
        link(dve.tensor_tensor(eq[:, :, :], e_in[:, :, :], wide(m1), ALU.is_equal))
        first_of(oh1, eq)
        link(dve.scalar_tensor_tensor(out=e2[:, :, :], in0=oh1[:, :, :], scalar=-3e38, in1=e_in[:, :, :], op0=MUL, op1=ADD))
        link(dve.tensor_reduce(m2[:, :], e2[:, :, :], AX.X, ALU.max))
        dve.tensor_tensor(pe2[:, :], m2[:, :], m1[:, :], SUB).then_inc(gsub_made, 1)
        link(dve.tensor_tensor(eq[:, :, :], e2[:, :, :], wide(m2), ALU.is_equal))
        first_of(oh2, eq)
        for A, o in ((A1, oh1), (A2, oh2)):
            link(dve.tensor_tensor(A[:, :, :, :], oh[:, :, :].unsqueeze(3).broadcast_to([P, TT, NG, EPG]),
                                   o[:, :, :].unsqueeze(2).broadcast_to([P, TT, NG, EPG]), MUL))
        dve.tensor_tensor(AA[:, :, :, :], A1[:, :, :, :], A2[:, :, :, :], ADD).then_inc(A_made, 1)
        dve.wait_ge(gexp_made, 1)
        link(dve.tensor_reduce(gw[:, :], ge4[:, :, :], AX.X, ADD))
        link(dve.reciprocal(gw[:, :], gw[:, :]))
        dve.wait_ge(gexp_made, 2)
        link(dve.tensor_scalar(rden2[:, :], pe2[:, :], 1.0, None, ADD))
        link(dve.reciprocal(rden2[:, :], rden2[:, :]))
        link(dve.tensor_tensor(gates[:, 0, :], rden2[:, :], gw[:, :], MUL))
        dve.tensor_tensor(gates[:, 1, :], gates[:, 0, :], pe2[:, :], MUL)
        dve.wait_ge(rank_ps, 1)
        link(dve.tensor_copy(tot[:, :, :], bank(1, 128, 128 + TT * NE).rearrange("p (t n) -> p t n", t=TT)))
        link(dve.memset(bt[:, 0, :], 0.0))
        for t in range(1, TT):
            link(dve.tensor_tensor(bt[:, t, :], bt[:, t - 1, :], tot[:, t - 1, :], ADD))
        link(dve.tensor_tensor(cnt[:, :], bt[:, TT - 1, :], tot[:, TT - 1, :], ADD))
        link(dve.tensor_tensor(rank[:, :, :], bank(1, 0, TT * NE).rearrange("p (t n) -> p t n", t=TT), bt[:, :, :], ADD))
        for s in range(2):
            link(dve.memset(cum[s][:, 0:8], 0.0))
        ovf_n = cum[0][:, 8:24]
        link(dve.tensor_scalar(ovf_n, cnt[:, :], 128.5, None, ALU.is_ge))
        for m in range(2, TT):
            link(dve.scalar_tensor_tensor(out=ovf_n, in0=cnt[:, :], scalar=m * P + 0.5, in1=ovf_n, op0=ALU.is_ge, op1=ADD))
        link(dve.tensor_copy(n_ov[:, :], ovf_n))
        for n, d in enumerate((1, 2, 4, 8)):
            a, b = cum[n % 2], cum[1 - n % 2]
            link(dve.tensor_tensor(b[:, 8:24], a[:, 8:24], a[:, 8 - d:24 - d], ADD))
        ov_incl = cum[0][:, 8:24]
        link(dve.tensor_scalar(ovf[:, :], rt[:, R_IOTA:R_IOTA + N_OV], ov_incl[:, NE - 1:NE], None, ALU.is_lt))
        link(dve.tensor_reduce(npf[:, :], ovf[:, :].rearrange("p (o a) -> p a o", a=2)[:, 0:1, :], AX.X, ADD))
        link(dve.tensor_scalar(npf[:, :], npf[:, :], NE / 2 - 1.0, None, ADD))
        dve.tensor_copy(npi[:, :], npf[:, :])
        link(dve.tensor_tensor(ovt[:, :, :], ov_incl.unsqueeze(1).broadcast_to([P, N_OV, NE]),
                               rt[:, R_IOTA:R_IOTA + N_OV].unsqueeze(2).broadcast_to([P, N_OV, NE]), ALU.is_le))
        link(dve.tensor_reduce(ovf[:, :], ovt[:, :, :], AX.X, ADD))
        link(dve.tensor_scalar(ovf[:, :], ovf[:, :], float(NE - 1), None, ALU.min))
        dve.tensor_copy(tile_e[:, NE:NTILE], ovf[:, :])
        dve.memset(tile_e[:, NTILE:NTILE + 2], 0)
        dve.tensor_copy(tile_e[:, 0:NE], rt[:, R_E:R_E + NE]).then_inc(np_made, 1)
        link(dve.tensor_scalar(fl[:, :, :], rank[:, :, :], float(P), None, ALU.is_ge))
        for m in range(2, TT):
            link(dve.scalar_tensor_tensor(out=fl[:, :, :], in0=rank[:, :, :], scalar=float(m * P), in1=fl[:, :, :], op0=ALU.is_ge, op1=ADD))
        link(dve.tensor_tensor(c1[:, :], ov_incl, n_ov[:, :], SUB))
        link(dve.tensor_tensor(c1[:, :], c1[:, :], rt[:, R_E:R_E + NE], SUB))
        link(dve.tensor_scalar(c1[:, :], c1[:, :], float(NE - 1), None, ADD))
        link(dve.tensor_scalar(smap[:, :, :], fl[:, :, :], 1.0, None, ALU.is_ge))
        link(dve.tensor_tensor(smap[:, :, :], smap[:, :, :], c1[:, :].unsqueeze(1).broadcast_to([P, TT, NE]), MUL))
        link(dve.scalar_tensor_tensor(out=smap[:, :, :], in0=fl[:, :, :], scalar=1.0 - P * NTILE, in1=smap[:, :, :], op0=MUL, op1=ADD))
        link(dve.scalar_tensor_tensor(out=smap[:, :, :], in0=rank[:, :, :], scalar=float(NTILE), in1=smap[:, :, :], op0=MUL, op1=ADD))
        link(dve.tensor_tensor(smap[:, :, :], smap[:, :, :], rt[:, R_E:R_E + NE].unsqueeze(1).broadcast_to([P, TT, NE]), ADD))
        for a, A in enumerate((A1, A2)):
            flat = A[:, :, :, :].rearrange("p t g e -> p t (g e)")
            link(dve.tensor_tensor(flat, flat, smap[:, :, :], MUL))
            link(dve.tensor_reduce(posf[:, a, :], flat, AX.X, ADD))
        dve.tensor_copy(slots[:, :, :], posf[:, :, :]).then_inc(slots_made, 1)

        def gate_up_lo(q, n, u):
            dve.wait_ge((g_hi, u_hi)[u], n + 1)
            cols = slice(u * FF, (u + 1) * FF)
            dve.tensor_tensor(gu_lo[q][:, :, cols], m_raw[3 * q + u][:, :].rearrange("p (k n) -> p k n", k=KB),
                              gu_hi[q][:, :, cols].bitcast(f32), SUB).then_inc((g_lo, u_lo)[u], 1)

        def tokens_lo(n, q):
            dve.wait_ge(xt_hi, n + 1)
            dve.tensor_tensor(xt_l[q][:, :, :].rearrange("p k n -> p (k n)"), pair(0, D),
                              xt_h[q][:, :, :].rearrange("p k n -> p (k n)").bitcast(f32), SUB).then_inc(xt_lo, 1)

        def head(i, q, more):
            dve.wait_ge(sg_made, i + 1)
            dve.tensor_tensor(hid[:, :], sg[:, :], bank(2 + q, FF, 2 * FF), MUL).then_inc(hid_made, 1)
            if more:
                tokens_lo(i + 1, 1 - q)
            dve.wait_ge(ht_hi, i + 1)
            dve.tensor_tensor(ht_l[q][:, :, :].rearrange("p f n -> p (f n)"), bank(4, 0, FF),
                              ht_h[q][:, :, :].rearrange("p f n -> p (f n)").bitcast(f32), SUB).then_inc(ht_lo, 1)

        def tail(i, r, q):
            dve.wait_ge(dn_ps, i + 1)
            dve.wait_ge(y_sent[q], r * 16 + 16)
            dve.tensor_copy(ys[q][:, 512:D], bank(7)).then_inc(ys_b, 1)

        dve.wait_ge(np_made, 1)
        last = dve.value_load(npi[0:1, 0:1], min_val=NE // 2 - 1, max_val=(NE + 8) // 2)
        gate_up_lo(1, 1, 0)
        gate_up_lo(1, 1, 1)
        tokens_lo(0, 0)
        head(0, 0, True)
        gate_up_lo(0, 2, 0)
        with dve.Fori(0, last) as r:
            for q in range(2):
                gate_up_lo(q, r * 2 + (q + 2), 1)
                head(r * 2 + (q + 1), 1 - q, True)
                gate_up_lo(1 - q, r * 2 + (q + 3), 0)
                tail(r * 2 + q, r, q)
        head(last * 2 + 1, 1, False)
        tail(last * 2, last, 0)
        tail(last * 2 + 1, last, 1)

        def combine(t):
            cnd = 0 if t < LT else 1
            dve.wait_ge(ya_scaled, t + 1)
            link(dve.scalar_tensor_tensor(out=ya[t][:, :], in0=yb[t][:, :], scalar=gates[:, 1, t:t + 1], in1=ya[t][:, :], op0=MUL, op1=ADD))
            dve.tensor_tensor(ya[t][:, :], ya[t][:, :], g2t[:, cnd, :], MUL).then_inc(y_made, 1)

        def finish(t):
            col = slice(t, t + 1)
            dve.wait_ge(sq_made, 2 * TT + t + 1)
            dve.tensor_scalar(var_x[:, col], ss[:, col], 1.0 / D, EPS, MUL, ADD).then_inc(var_made, 1)
            dve.wait_ge(rs_raw, 3 + t)
            refine(rs_x[:, col], var_x[:, col], nw[:, col])
            if t >= 2:
                dve.wait_ge(yo_sent[t % 2], 16 * (t // 2))
            dve.scalar_tensor_tensor(out=yo[t % 2][:, :], in0=x[:, t, :], scalar=rs_x[:, col], in1=fint[:, :], op0=MUL, op1=MUL).then_inc(yo_made, 1)

        combine(0)
        combine(1)
        for t in range(TT):
            if t + 2 < TT:
                combine(t + 2)
            finish(t)

    ctx.close()


def constants():
    p = np.arange(P)
    cst = np.zeros((P, N_CST), np.float32)
    cst[:, C_ID:C_ID + P] = np.eye(P)
    ang = 2 * np.pi * np.outer(p, p) / P
    cst[:, C_DCH:C_DCH + P] = np.cos(ang)
    cst[:, C_DCH + P:C_DCH + 2 * P] = -np.sin(ang)
    cst[:, C_DPR:C_DPR + P] = np.cos(ang) / P
    cst[:, C_DPR + P:C_DPR + 2 * P] = np.sin(ang) / P
    for g, w in enumerate(WINDOWS):
        n = w // 2
        for q in range(4):
            length = N_LAT if q < 2 else N_CTX
            for i in range(n):
                t = i if q % 2 == 0 else length - n + i
                cnt = min(t + w - n, length) - max(t - n, 0)
                cst[:, C_EDGE + (g * 4 + q) * 8 + i] = w / cnt
    rt = np.zeros((P, N_RT), np.float32)
    rt[:, R_U:R_U + P] = p[:, None] < p[None, :]
    rt[:, R_TID:R_TID + TT] = p[:, None] + P * np.arange(TT)
    rt[:, R_E:R_E + NE] = np.arange(NE)
    rt[:, R_IOTA:R_IOTA + N_OV] = np.arange(N_OV)
    n = np.arange(N_LAT)
    inv = (np.float32(10000.0) ** (-np.arange(HD // 4, dtype=np.float32) / np.float32(HD // 4))).astype(np.float32)
    ang = np.concatenate([(n // 64).astype(np.float32)[:, None] * inv, (n % 64).astype(np.float32)[:, None] * inv], axis=1)
    rope = np.concatenate([np.cos(ang), np.sin(ang)], axis=1).astype(np.float32)
    th = 2 * np.pi * (np.outer(n, n) % N_LAT) / N_LAT
    scale = 1.0 / np.sqrt(N_LAT * P)
    dft = np.concatenate([np.cos(th) * scale, np.sin(th) * scale], axis=1).astype(np.float32)
    return {"cst": cst, "rt": rt, "rope": rope, "dft": dft}


_INS = ['x_prompt', 'x_sample', 'cache_k', 'cache_v', 'c', 'c_ctx', 'w_ada', 'b_ada', 'norm_mix', 'norm_ffn', 'w_in',
        'w_out', 'q_norm', 'k_norm', 'conv_w', 'conv_b', 'conv_ln_g', 'conv_ln_b', 'pool_w', 'pool_scale',
        'router_group_w', 'router_group_b', 'router_expert_w', 'router_expert_b', 'moe_w_gate', 'moe_w_up',
        'moe_w_down', 'final_norm']
_OUTS = [(1, N_CTX, D), (1, N_LAT, D), (1, 1, N_CTX, KV, HD), (1, 1, N_CTX, KV, HD)]


def kernel(**inputs):
    import concourse.bacc as _bacc
    from concourse.bass_utils import run_bass_kernel_spmd as _run

    nc = _bacc.Bacc("TRN2", target_bir_lowering=False, num_devices=1)
    arrays, args = {}, []
    tables = constants()
    for name, a in [(n, inputs[n]) for n in _INS] + list(tables.items()):
        a = np.ascontiguousarray(a)
        arrays[f"in_{name}_dram"] = a
        args.append(nc.dram_tensor(f"in_{name}_dram", a.shape, mybir.dt.from_np(a.dtype), kind="ExternalInput").ap())
    for i, shape in enumerate(_OUTS):
        args.append(nc.dram_tensor(f"out_{i}_dram", shape, mybir.dt.float32, kind="ExternalOutput").ap())
    for name, shape, dt in (("mod_rows", (2, 4 * D), mybir.dt.float32), ("h2_rows", (TOK, D), mybir.dt.float32),
                            ("slot_list", (P * NTILE, 1), mybir.dt.int32), ("y_rows", (P * NTILE, D), mybir.dt.float32)):
        args.append(nc.dram_tensor(name, shape, dt, kind="Internal").ap())
    build(nc, *args)
    r = _run(nc, [arrays], core_ids=[0])
    return tuple(r.results[0][f"out_{i}_dram"] for i in range(len(_OUTS)))
```
